# Optimizing a Trainium2 kernel written in Bass

```python
import numpy as np
import jax
import jax.numpy as jnp
from jax import lax

D_MODEL = 1024
BATCH = 1
SEQ = 2048
DEPTH = 1

PLE_DIM = 256
N_HEADS = 8
N_KV = 2
HPG = N_HEADS // N_KV
HEAD_DIM = 64
CMP_BLOCK = 32
CMP_STRIDE = 16
CMP_HIDDEN = 128
SEL_BLOCK = 64
N_SEL = 8
WINDOW = 512
Q_BLOCK = 128
SEL_Q_BLOCK = 32
CONV_CH = 512
CONV_WIDTH = 31
N_GROUPS = 4
EXP_PER_GROUP = 8
N_EXPERTS = N_GROUPS * EXP_PER_GROUP
EXPERT_FF = 512
TOP_K = 2
MOE_BLOCK = 128
EPS = 1e-6
NEG = -1e30
BIG = 1e4
Q_COLS = N_HEADS * HEAD_DIM
KV_COLS = N_KV * HEAD_DIM
OFF_KV = Q_COLS
OFF_GATE = OFF_KV + 6 * KV_COLS
OFF_CONV = OFF_GATE + 3 * N_HEADS
OFF_MERGE = OFF_CONV + 2 * CONV_CH
N_IN = OFF_MERGE + 2 * D_MODEL

kernel_name = "hybrid_nsa_conformer_hmoe_block"

def rmsnorm(x, g):
    xf = x.astype(jnp.float32)
    y = xf * lax.rsqrt(jnp.mean(xf * xf, axis=-1, keepdims=True) + EPS)
    return (y * g.astype(jnp.float32)).astype(x.dtype)

def masked_softmax(s, mask):
    p = jax.nn.softmax(jnp.where(mask, s, NEG), axis=-1)
    return jnp.where(mask, p, 0.0)

def alibi_slopes():
    m = 2.0 ** (-8.0 * np.arange(1, N_HEADS + 1) / N_HEADS)
    return jnp.asarray(m.reshape(N_KV, HPG), jnp.float32)

def compress(kv_raw, pe, w1, w2):
    b, s, g, dh = kv_raw.shape
    nc = (s - CMP_BLOCK) // CMP_STRIDE + 1
    idx = np.arange(nc)[:, None] * CMP_STRIDE + np.arange(CMP_BLOCK)[None, :]
    blk = kv_raw[:, idx] + pe[None, None, :, None, :]
    blk = blk.transpose(0, 1, 3, 2, 4).reshape(b, nc, g, CMP_BLOCK * dh)
    return jax.nn.gelu(blk @ w1) @ w2

def nsa(q, kc, vc, ks, vs, kw, vw, gates, slopes):
    b, s = q.shape[0], q.shape[1]
    scale = HEAD_DIM ** -0.5
    nc = kc.shape[1]
    nsb = s // SEL_BLOCK
    n_sel = min(N_SEL, nsb)
    c_end = jnp.arange(nc, dtype=jnp.int32) * CMP_STRIDE + CMP_BLOCK - 1
    c_start_np = np.arange(nc) * CMP_STRIDE
    s_start_np = np.arange(nsb) * SEL_BLOCK
    overlap = jnp.asarray((c_start_np[:, None] < s_start_np[None, :] + SEL_BLOCK)
                          & (c_start_np[:, None] + CMP_BLOCK > s_start_np[None, :]), jnp.float32)
    blk_ids = jnp.arange(nsb, dtype=jnp.int32)

    def cmp_block(j):
        q0 = j * Q_BLOCK
        t = q0 + jnp.arange(Q_BLOCK, dtype=jnp.int32)
        qb = lax.dynamic_slice_in_dim(q, q0, Q_BLOCK, axis=1)
        sc = jnp.einsum('bqgrd,bngd->bgrqn', qb, kc).astype(jnp.float32) * scale
        dist = (t[:, None] - c_end[None, :]).astype(jnp.float32)
        sc = sc - slopes[None, :, :, None, None] * dist
        pc = masked_softmax(sc, (c_end[None, :] <= t[:, None]))
        oc = jnp.einsum('bgrqn,bngd->bqgrd', pc.astype(vc.dtype), vc)
        imp = jnp.einsum('bgrqn,nj->bgqj', pc, overlap)
        valid = (blk_ids[None, :] * SEL_BLOCK) <= t[:, None]
        cur = t[:, None] // SEL_BLOCK
        forced = (blk_ids[None, :] == 0) | (blk_ids[None, :] == cur) | (blk_ids[None, :] == cur - 1)
        score = jnp.where(valid, imp + jnp.where(forced, BIG, 0.0), -BIG)
        top, idx = lax.top_k(score, n_sel)
        ok = top > -0.5 * BIG
        return oc, idx.transpose(0, 2, 1, 3), ok.transpose(0, 2, 1, 3)

    o_c, sel_idx, sel_ok = lax.map(cmp_block, jnp.arange(s // Q_BLOCK, dtype=jnp.int32))
    o_c = jnp.moveaxis(o_c, 0, 1).reshape(b, s, N_KV, HPG, HEAD_DIM)
    sel_idx = jnp.moveaxis(sel_idx, 0, 1).reshape(b, s, N_KV, n_sel)
    sel_ok = jnp.moveaxis(sel_ok, 0, 1).reshape(b, s, N_KV, n_sel)

    ksb = ks.reshape(b, nsb, SEL_BLOCK, N_KV, HEAD_DIM).transpose(0, 3, 1, 2, 4)
    vsb = vs.reshape(b, nsb, SEL_BLOCK, N_KV, HEAD_DIM).transpose(0, 3, 1, 2, 4)
    b_ix = jnp.arange(b)[:, None, None, None]
    g_ix = jnp.arange(N_KV)[None, None, :, None]

    def sel_block(j):
        q0 = j * SEL_Q_BLOCK
        t = q0 + jnp.arange(SEL_Q_BLOCK, dtype=jnp.int32)
        qb = lax.dynamic_slice_in_dim(q, q0, SEL_Q_BLOCK, axis=1)
        idx = lax.dynamic_slice_in_dim(sel_idx, q0, SEL_Q_BLOCK, axis=1)
        ok = lax.dynamic_slice_in_dim(sel_ok, q0, SEL_Q_BLOCK, axis=1)
        kg = ksb[b_ix, g_ix, idx]
        vg = vsb[b_ix, g_ix, idx]
        kpos = idx[..., None] * SEL_BLOCK + jnp.arange(SEL_BLOCK, dtype=jnp.int32)
        tt = t[None, :, None, None, None]
        mask = ((kpos <= tt) & ok[..., None])[:, :, :, None]
        dist = (tt - kpos).astype(jnp.float32)[:, :, :, None]
        ss = jnp.einsum('bqgrd,bqgnkd->bqgrnk', qb, kg).astype(jnp.float32) * scale
        ss = ss - slopes[None, None, :, :, None, None] * dist
        m = n_sel * SEL_BLOCK
        ps = masked_softmax(ss.reshape(b, SEL_Q_BLOCK, N_KV, HPG, m), mask.reshape(b, SEL_Q_BLOCK, N_KV, 1, m))
        return jnp.einsum('bqgrm,bqgmd->bqgrd', ps.astype(vg.dtype), vg.reshape(b, SEL_Q_BLOCK, N_KV, m, HEAD_DIM))

    o_s = lax.map(sel_block, jnp.arange(s // SEL_Q_BLOCK, dtype=jnp.int32))
    o_s = jnp.moveaxis(o_s, 0, 1).reshape(b, s, N_KV, HPG, HEAD_DIM)

    kwp = jnp.pad(kw, ((0, 0), (WINDOW, 0), (0, 0), (0, 0)))
    vwp = jnp.pad(vw, ((0, 0), (WINDOW, 0), (0, 0), (0, 0)))

    def win_block(j):
        q0 = j * Q_BLOCK
        t = q0 + jnp.arange(Q_BLOCK, dtype=jnp.int32)
        qb = lax.dynamic_slice_in_dim(q, q0, Q_BLOCK, axis=1)
        kb = lax.dynamic_slice_in_dim(kwp, q0, WINDOW + Q_BLOCK, axis=1)
        vb = lax.dynamic_slice_in_dim(vwp, q0, WINDOW + Q_BLOCK, axis=1)
        kpos = q0 - WINDOW + jnp.arange(WINDOW + Q_BLOCK, dtype=jnp.int32)
        d = t[:, None] - kpos[None, :]
        mask = (d >= 0) & (d < WINDOW) & (kpos[None, :] >= 0)
        sw = jnp.einsum('bqgrd,bkgd->bgrqk', qb, kb).astype(jnp.float32) * scale
        sw = sw - slopes[None, :, :, None, None] * d.astype(jnp.float32)
        pw = masked_softmax(sw, mask)
        return jnp.einsum('bgrqk,bkgd->bqgrd', pw.astype(vb.dtype), vb)

    o_w = lax.map(win_block, jnp.arange(s // Q_BLOCK, dtype=jnp.int32))
    o_w = jnp.moveaxis(o_w, 0, 1).reshape(b, s, N_KV, HPG, HEAD_DIM)

    o = gates[..., 0:1] * o_c + gates[..., 1:2] * o_s + gates[..., 2:3] * o_w
    return o.reshape(b, s, N_HEADS * HEAD_DIM)

def conformer_conv(u, conv_w, conv_b, ln_g, ln_b, w_out):
    a, g = jnp.split(u, 2, axis=-1)
    z = a * jax.nn.sigmoid(g)
    zp = jnp.pad(z, ((0, 0), (CONV_WIDTH - 1, 0), (0, 0)))
    z = lax.conv_general_dilated(zp, conv_w[:, None, :].astype(zp.dtype), (1,), 'VALID',
                                 dimension_numbers=('NWC', 'WIO', 'NWC'),
                                 feature_group_count=CONV_CH) + conv_b
    zf = z.astype(jnp.float32)
    mu = jnp.mean(zf, axis=-1, keepdims=True)
    var = jnp.mean(jnp.square(zf - mu), axis=-1, keepdims=True)
    z = ((zf - mu) * lax.rsqrt(var + EPS) * ln_g.astype(jnp.float32) + ln_b.astype(jnp.float32)).astype(u.dtype)
    return jax.nn.silu(z) @ w_out

def hier_moe(h, w_rg, b_rg, w_re, b_re, w_g, w_u, w_d):
    b, s, d = h.shape
    t_n = b * s
    hf = h.reshape(t_n, d)
    lg = (hf @ w_rg).astype(jnp.float32) + b_rg.astype(jnp.float32)
    pg = jax.nn.softmax(lg, axis=-1)
    gsel = jnp.argmax(lg, axis=-1).astype(jnp.int32)
    pg_sel = jnp.take_along_axis(pg, gsel[:, None], axis=1)
    le = ((hf @ w_re).astype(jnp.float32) + b_re.astype(jnp.float32)).reshape(t_n, N_GROUPS, EXP_PER_GROUP)
    le_g = jnp.take_along_axis(le, gsel[:, None, None], axis=1)[:, 0]
    top, loc = lax.top_k(jax.nn.softmax(le_g, axis=-1), TOP_K)
    wts = pg_sel * top / jnp.sum(top, axis=-1, keepdims=True)
    eid = gsel[:, None] * EXP_PER_GROUP + loc.astype(jnp.int32)
    tk = t_n * TOP_K
    flat_e = eid.reshape(tk)
    flat_tok = jnp.repeat(jnp.arange(t_n, dtype=jnp.int32), TOP_K)
    flat_w = wts.reshape(tk)
    order = jnp.argsort(flat_e)
    se, stok, sw = flat_e[order], flat_tok[order], flat_w[order]
    counts = jnp.bincount(flat_e, length=N_EXPERTS).astype(jnp.int32)
    starts = jnp.cumsum(counts) - counts
    padded = (counts + MOE_BLOCK - 1) // MOE_BLOCK * MOE_BLOCK
    pends = jnp.cumsum(padded)
    pstarts = pends - padded
    dest = pstarts[se] + jnp.arange(tk, dtype=jnp.int32) - starts[se]
    n_blk = -(-(tk + N_EXPERTS * (MOE_BLOCK - 1)) // MOE_BLOCK)
    p_rows = n_blk * MOE_BLOCK
    buf_tok = jnp.full((p_rows,), t_n, jnp.int32).at[dest].set(stok)
    buf_w = jnp.zeros((p_rows,), jnp.float32).at[dest].set(sw)
    blk_e = jnp.minimum(jnp.searchsorted(pends, jnp.arange(n_blk, dtype=jnp.int32) * MOE_BLOCK, side='right'),
                        N_EXPERTS - 1).astype(jnp.int32)
    hp = jnp.concatenate([hf, jnp.zeros((1, d), hf.dtype)], axis=0)

    def expert_block(args):
        tok, w, e = args
        xb = hp[tok]
        y = (jax.nn.silu(xb @ w_g[e]) * (xb @ w_u[e])) @ w_d[e]
        return y * w[:, None].astype(y.dtype)

    yb = lax.map(expert_block, (buf_tok.reshape(n_blk, MOE_BLOCK), buf_w.reshape(n_blk, MOE_BLOCK), blk_e))
    y = jnp.zeros((t_n + 1, d), yb.dtype).at[buf_tok].add(yb.reshape(p_rows, d))[:t_n]
    return y.reshape(b, s, d).astype(h.dtype)

def setup_inputs(seed: int = 0) -> dict:
    key = jax.random.key(seed)
    ks = jax.random.split(key, 32)
    f32 = jnp.float32

    def nrm(k, shape, scale):
        return jax.random.normal(k, shape, f32) * scale

    def gain(k, shape):
        return 1.0 + 0.02 * jax.random.normal(k, shape, f32)

    L = DEPTH
    return {
        "x": nrm(ks[0], (BATCH, SEQ, D_MODEL), 1.0),
        "p": nrm(ks[1], (DEPTH, BATCH, SEQ, PLE_DIM), 1.0),
        "attn_norm_g": gain(ks[2], (L, D_MODEL)),
        "w_in": nrm(ks[3], (L, D_MODEL, N_IN), D_MODEL ** -0.5),
        "q_norm_g": gain(ks[4], (L, HEAD_DIM)),
        "k_norm_g": gain(ks[5], (L, 3, HEAD_DIM)),
        "cmp_pos": nrm(ks[6], (L, 2, CMP_BLOCK, HEAD_DIM), 0.1),
        "cmp_w1": nrm(ks[7], (L, 2, CMP_BLOCK * HEAD_DIM, CMP_HIDDEN), (CMP_BLOCK * HEAD_DIM) ** -0.5),
        "cmp_w2": nrm(ks[8], (L, 2, CMP_HIDDEN, HEAD_DIM), CMP_HIDDEN ** -0.5),
        "w_attn_out": nrm(ks[9], (L, N_HEADS * HEAD_DIM, D_MODEL), (N_HEADS * HEAD_DIM) ** -0.5),
        "conv_w": nrm(ks[10], (L, CONV_WIDTH, CONV_CH), CONV_WIDTH ** -0.5),
        "conv_b": nrm(ks[11], (L, CONV_CH), 0.02),
        "conv_norm_g": gain(ks[12], (L, CONV_CH)),
        "conv_norm_b": nrm(ks[13], (L, CONV_CH), 0.02),
        "w_conv_out": nrm(ks[14], (L, CONV_CH, D_MODEL), CONV_CH ** -0.5),
        "merge_b": nrm(ks[15], (L, 2 * D_MODEL), 0.02),
        "w_out": nrm(ks[16], (L, D_MODEL, D_MODEL), D_MODEL ** -0.5),
        "ffn_norm_g": gain(ks[17], (L, D_MODEL)),
        "w_router_group": nrm(ks[18], (L, D_MODEL, N_GROUPS), D_MODEL ** -0.5),
        "b_router_group": nrm(ks[19], (L, N_GROUPS), 0.01),
        "w_router_expert": nrm(ks[20], (L, D_MODEL, N_EXPERTS), D_MODEL ** -0.5),
        "b_router_expert": nrm(ks[21], (L, N_EXPERTS), 0.01),
        "w_exp_gate": nrm(ks[22], (L, N_EXPERTS, D_MODEL, EXPERT_FF), D_MODEL ** -0.5),
        "w_exp_up": nrm(ks[23], (L, N_EXPERTS, D_MODEL, EXPERT_FF), D_MODEL ** -0.5),
        "w_exp_down": nrm(ks[24], (L, N_EXPERTS, EXPERT_FF, D_MODEL), EXPERT_FF ** -0.5),
        "ple_norm_g": gain(ks[25], (L, D_MODEL)),
        "w_ple_gate": nrm(ks[26], (L, D_MODEL, D_MODEL), D_MODEL ** -0.5),
        "b_ple_gate": nrm(ks[27], (L, D_MODEL), 0.02),
        "w_ple_proj": nrm(ks[28], (L, PLE_DIM, D_MODEL), PLE_DIM ** -0.5),
    }

def reference(x, p, attn_norm_g, w_in, q_norm_g, k_norm_g, cmp_pos, cmp_w1, cmp_w2, w_attn_out,
              conv_w, conv_b, conv_norm_g, conv_norm_b, w_conv_out, merge_b, w_out,
              ffn_norm_g, w_router_group, b_router_group, w_router_expert, b_router_expert,
              w_exp_gate, w_exp_up, w_exp_down, ple_norm_g, w_ple_gate, b_ple_gate, w_ple_proj):
    b, s, _ = x.shape
    slopes = alibi_slopes()
    for i in range(DEPTH):
        h = rmsnorm(x, attn_norm_g[i])
        z = h @ w_in[i]
        q = rmsnorm(z[..., :Q_COLS].reshape(b, s, N_KV, HPG, HEAD_DIM), q_norm_g[i])
        kv = z[..., OFF_KV:OFF_GATE].reshape(b, s, 6, N_KV, HEAD_DIM)
        kc = rmsnorm(compress(kv[:, :, 0], cmp_pos[i, 0], cmp_w1[i, 0], cmp_w2[i, 0]), k_norm_g[i, 0])
        vc = compress(kv[:, :, 1], cmp_pos[i, 1], cmp_w1[i, 1], cmp_w2[i, 1])
        k_sel = rmsnorm(kv[:, :, 2], k_norm_g[i, 1])
        k_win = rmsnorm(kv[:, :, 4], k_norm_g[i, 2])
        nsa_gates = jax.nn.sigmoid(z[..., OFF_GATE:OFF_CONV].reshape(b, s, N_KV, HPG, 3))
        attn = nsa(q, kc, vc, k_sel, kv[:, :, 3], k_win, kv[:, :, 5], nsa_gates, slopes)
        y_a = attn @ w_attn_out[i]
        y_c = conformer_conv(z[..., OFF_CONV:OFF_MERGE], conv_w[i], conv_b[i], conv_norm_g[i],
                             conv_norm_b[i], w_conv_out[i])
        mg = jax.nn.sigmoid(z[..., OFF_MERGE:] + merge_b[i])
        x = x + (mg[..., :D_MODEL] * y_a + mg[..., D_MODEL:] * y_c) @ w_out[i]
        x = x + hier_moe(rmsnorm(x, ffn_norm_g[i]), w_router_group[i], b_router_group[i],
                         w_router_expert[i], b_router_expert[i], w_exp_gate[i], w_exp_up[i], w_exp_down[i])
        gate = jax.nn.sigmoid(rmsnorm(x, ple_norm_g[i]) @ w_ple_gate[i] + b_ple_gate[i])
        x = x + gate * (p[i] @ w_ple_proj[i])
    return x


_drawn_inputs = setup_inputs


def setup_inputs(seed=0):
    import zlib

    import numpy as np

    out = dict(_drawn_inputs(seed))
    spreads = {}
    factors = {'attn_norm_g': 3.043,
     'q_norm_g': 7.689,
     'k_norm_g': 8.0,
     'conv_b': 2.71,
     'conv_norm_g': 13.408,
     'conv_norm_b': 14.16,
     'merge_b': 6.116,
     'b_router_group': 26.565,
     'b_router_expert': 24.49,
     'ple_norm_g': 64.0,
     'b_ple_gate': 64.0,
     'ffn_norm_g': 4.796}
    for name, (base, spread) in spreads.items():
        noise = np.random.default_rng([zlib.crc32(name.encode()), seed]).standard_normal(out[name].shape)
        drawn = base * np.exp(spread * noise) if base else spread * noise
        out[name] = jnp.asarray(drawn.astype(out[name].dtype))
    for name, factor in factors.items():
        out[name] = (out[name] * factor).astype(out[name].dtype)
    return out
```

```python
from contextlib import ExitStack

import concourse.bass as bass
from concourse import mybir

F32 = mybir.dt.float32
BF16 = mybir.dt.bfloat16
F32R = mybir.dt.float32r
I32 = mybir.dt.int32
U32 = mybir.dt.uint32
ALU = mybir.AluOpType
ACT = mybir.ActivationFunctionType
AX = mybir.AxisListType.X
ts, ds = bass.ts, bass.ds

P = 128
SEQ = 2048
NT = SEQ // P
D = 1024
KD = D // P
PLE = 256
NH, NKV, HD = 8, 2, 64
HPG = NH // NKV
CMP_BLOCK, CMP_STRIDE, CMP_HID = 32, 16, 128
NC = (SEQ - CMP_BLOCK) // CMP_STRIDE + 1
SEL_BLOCK, N_SEL = 64, 8
NSB = SEQ // SEL_BLOCK
WINDOW = 512
CONV, CW = 512, 31
HALO = CW - 1
NCH = CONV // P
NG, EPG = 4, 8
NE = NG * EPG
FF = 512
KF = FF // P
EPS = 1e-6
NEG = -1e30
BIG = 1e4
Q_COLS = NH * HD
KV_COLS = NKV * HD
OFF_GATE = Q_COLS + 6 * KV_COLS
OFF_CONV = OFF_GATE + 3 * NH
OFF_MERGE = OFF_CONV + 2 * CONV
N_IN = OFF_MERGE + 2 * D
MAX_BLK = (2 * SEQ + NE * P) // P
SCALE = HD ** -0.5
AUG = HD + 2
ZT_COLS = HALO + SEQ + P
QB = 512
NEGC = 120


class Chain:

    def __init__(self, eng, sem):
        self.eng, self.sem, self.n = eng, sem, 0

    def mark(self, ins):
        self.n += 1
        ins.then_inc(self.sem, 1)
        return ins

    def sync(self, back=0):
        if self.n > back:
            self.eng.wait_ge(self.sem, self.n - back)

    def restart(self):
        self.sync()
        self.eng.sem_clear(self.sem)
        self.n = 0

    def close(self):
        self.sync()


def tiles(eng, chain, step, last=NT):
    step(0)
    chain.restart()
    with eng.Fori(1, last - 1) as j:
        step(j)
        chain.restart()
    step(last - 1)


class Sems:

    def __init__(self, nc, ctx, tag):
        self.nc, self.tag, self.all = nc, tag, []
        ctx.callback(self.clear)

    def __call__(self, name):
        self.all.append(self.nc.alloc_semaphore(f"{self.tag}_{name}"))
        return self.all[-1]

    def clear(self):
        self.nc.clear_and_free_semaphores(self.all)
        self.nc.all_engine_barrier()


def bufs(nc, ctx, tag=""):
    def sb(name, shape, dt=F32, side=None):
        name = tag + name
        if side:
            return ctx.enter_context(nc.sbuf_tensor(name, shape, dt, side=side))
        return ctx.enter_context(nc.sbuf_tensor(name, shape, dt))

    def ps(name, shape, dt=F32):
        name = tag + name
        return ctx.enter_context(nc.psum_tensor(name, shape, dt))
    return sb, ps


KVB = Q_COLS + 4 * KV_COLS
CHUNKS = [(0, Q_COLS), (Q_COLS, 4 * KV_COLS), (KVB, OFF_CONV - KVB), (OFF_CONV + CONV, CONV), (OFF_CONV, CONV)]


def make_constants(nc, K):
    with ExitStack() as ctx:
        S = Sems(nc, ctx, "k")
        s_pool, s_dve, s_zero, s_pad = S("pool_chain"), S("dve_chain"), S("zero"), S("pads_stored")
        zrow = ctx.enter_context(nc.sbuf_tensor("zero_cols", [P, NCH, P], F32))
        block = ctx.enter_context(nc.Block())

        @block.gpsimd
        def _(pool):
            c = Chain(pool, s_pool)

            def put(ins):
                c.mark(ins)
                c.sync()
            for m in (K.ident, K.identb):
                put(nc.gpsimd.memset(m[:, :], 0.0))
                put(nc.gpsimd.affine_select(out=m[:, :], in_=m[:, :], compare_op=ALU.not_equal, fill=1.0,
                                            base=0, pattern=[[-1, P]], channel_multiplier=1))
            put(nc.gpsimd.iota(K.tpos[:, :], [[P, NT]], base=0, channel_multiplier=1,
                               allow_small_or_imprecise_dtypes=True))

        @block.vector
        def _(dve):
            c = Chain(dve, s_dve)
            nc.vector.memset(zrow[:, :, :], 0.0).then_inc(s_zero, 1)
            for t, v in ((K.kwinT[0:HD, :, 0:WINDOW], 0.0), (K.vwin[:, 0:WINDOW // P, :, 0:HD], 0.0),
                         (K.vwin[:, :, :, HD:HD + 1], 1.0), (K.vsel[:, :, :, HD:HD + 1], 1.0),
                         (K.vc[:, :, :], 0.0), (K.kcT[0:HD, :, NC:P], 0.0),
                         (K.mhalf[:, :], -0.5), (K.inv_d[:, :], 1.0 / D), (K.inv_hd[:, :], 1.0 / HD),
                         (K.forced[:, :], -1.0), (K.valid[:, :], -BIG)):
                c.mark(nc.vector.memset(t, v))
            for h in range(NH):
                c.mark(nc.vector.memset(K.nslope[:, h:h + 1], -(2.0 ** (-8.0 * (h + 1) / NH))))
            c.sync()
            for half in range(2):
                rows = slice(HD * half, HD * half + HD)
                c.mark(nc.vector.memset(K.forced[rows, NSB - 3 + half:NSB - 1 + half], BIG))
                c.mark(nc.vector.memset(K.valid[rows, 0:NSB - 1 + half], 3 * BIG))
            c.sync()

        @block.sync
        def _(sp):
            w_view = K.w_in[0].rearrange("(k p) n -> p k n", p=P)
            for n, (o, m) in enumerate(CHUNKS):
                sp.dma_start(K.w_proj[:, :, o:o + m], w_view[:, :, o:o + m]).then_inc(K.s_w[n], 16)
            sp.wait_ge(s_zero, 1)
            zt = K.zT_d.rearrange("(c p) t -> p c t", p=P)
            sp.dma_start(zt[:, :, 0:HALO], zrow[:, :, 0:HALO]).then_inc(s_pad, 16)
            sp.dma_start(zt[:, :, HALO + SEQ:ZT_COLS], zrow[:, :, :]).then_inc(s_pad, 16)
            sp.wait_ge(s_pad, 32)


def make_masks(nc, K, put):
    put(nc.gpsimd.memset(K.m_old[:, :], 0.0))
    put(nc.gpsimd.affine_select(out=K.m_old[:, :], in_=K.m_old[:, :], compare_op=ALU.is_gt, fill=NEG,
                                base=0, pattern=[[1, P]], channel_multiplier=-1))
    put(nc.gpsimd.memset(K.m_causal[:, :], 0.0))
    put(nc.gpsimd.affine_select(out=K.m_causal[:, :], in_=K.m_causal[:, :], compare_op=ALU.is_ge,
                                fill=NEG, base=QB - P, pattern=[[-1, 2 * QB - P]],
                                channel_multiplier=1))
    put(nc.gpsimd.memset(K.mT_old[:, :], 0.0))
    put(nc.gpsimd.affine_select(out=K.mT_old[:, :], in_=K.mT_old[:, :], compare_op=ALU.is_gt, fill=NEG,
                                base=0, pattern=[[-1, P]], channel_multiplier=1))
    put(nc.gpsimd.memset(K.mT_causal[:, :], 0.0))
    put(nc.gpsimd.affine_select(out=K.mT_causal[:, :], in_=K.mT_causal[:, :], compare_op=ALU.is_ge,
                                fill=NEG, base=P - QB, pattern=[[1, 2 * QB - P]],
                                channel_multiplier=-1))
    put(nc.gpsimd.memset(K.m_cmp[:, :], 0.0))
    put(nc.gpsimd.affine_select(out=K.m_cmp[:, :], in_=K.m_cmp[:, :], compare_op=ALU.is_ge, fill=NEG,
                                base=CMP_STRIDE * NEGC - (CMP_BLOCK - 1),
                                pattern=[[-CMP_STRIDE, NEGC + P]], channel_multiplier=1))
    put(nc.gpsimd.memset(K.has_cmp[:, :], 1.0))
    put(nc.gpsimd.affine_select(out=K.has_cmp[:, 0:1], in_=K.has_cmp[:, 0:1], compare_op=ALU.is_ge,
                                fill=0.0, base=-(CMP_BLOCK - 1), pattern=[[0, 1]],
                                channel_multiplier=1))
    def key_rows(buf, n, base, step, ones):
        r = buf[HD:96, :, :]
        put(nc.gpsimd.iota(r, [[0, NKV], [step, n]], base=base, channel_multiplier=0,
                           allow_small_or_imprecise_dtypes=True))
        put(nc.gpsimd.affine_select(out=r, in_=r, compare_op=ALU.is_equal, fill=0.0, base=0,
                                    pattern=[[0, NKV], [0, n]], channel_multiplier=1))
        for row in range(1, 1 + ones):
            put(nc.gpsimd.affine_select(out=r, in_=r, compare_op=ALU.not_equal, fill=1.0, base=-row,
                                        pattern=[[0, NKV], [0, n]], channel_multiplier=1))
    key_rows(K.kselT, SEQ, 0, 1, 2)
    key_rows(K.kwinT, WINDOW + SEQ, -WINDOW, 1, 2)
    key_rows(K.kcT, P, CMP_BLOCK - 1, CMP_STRIDE, 1)
    put(nc.gpsimd.memset(K.kwinT[HD:HD + 1, :, 0:WINDOW], NEG))
    r = K.kselT[96:P, :, :]
    put(nc.gpsimd.memset(r, 0.0))
    for g in range(NKV):
        rg = K.kselT[96:P, g, :].rearrange("p (b k) -> p b k", k=SEL_BLOCK)
        put(nc.gpsimd.affine_select(out=rg, in_=rg, compare_op=ALU.not_equal, fill=NEG, base=0,
                                    pattern=[[-1, NSB], [0, SEL_BLOCK]], channel_multiplier=1))


def project(nc, K):
    NN = NH + 2 * NKV
    with ExitStack() as ctx:
        sb, ps = bufs(nc, ctx, "a_")
        w, s_w = K.w_proj, K.s_w
        xt, h, hT = sb("x_rows", [P, D]), sb("h_rows", [P, D]), sb("hT", [P, KD, P])
        junk, gain = sb("squares_x", [P, D]), sb("gain_x", [P, D])
        gqk, gqk1 = sb("gain_qk", [P, NN, HD]), sb("gain_qk1", [P, 3, HD])
        sq, nrm = sb("squares_qk", [P, NN, HD]), sb("normed", [P, NN, HD])
        qrow, krow = sb("q_rows", [P, NH, AUG]), sb("k_rows", [P, 2, NKV * HD])
        kvraw = sb("kv_raw", [P, 2, NKV * HD])
        sg, zrow, zT = sb("glu_gate", [P, CONV]), sb("glu", [P, CONV]), sb("gluT", [P, NCH, P])
        ssq, ms, rstd = sb("ssq", [P, 1]), sb("ms", [P, 1]), sb("rstd", [P, 1])
        ss12, ms12, rr12 = sb("ssq_qk", [P, NN]), sb("ms_qk", [P, NN]), sb("rstd_qk", [P, NN])
        T = [ps(f"T{i}", [P, 4, P]) for i in range(2)]
        Z = [ps(f"Z{i}", [P, 512]) for i in range(5)]
        B = ps("B", [P, 4, P])
        S = Sems(nc, ctx, "a")
        s_gain, s_x, s_ssq, s_rstd, s_h = S("gain"), S("x"), S("ssq"), S("rstd"), S("h")
        s_th, s_hTe, s_hst, s_mm = S("hT_psum"), S("hT"), S("hT_stored"), S("z_psum")
        s_actz, s_dvez, s_sq, s_red, s_rr = S("z_read_act"), S("z_read_dve"), S("squares"), S("ssq_qk"), S("rr")
        s_q, s_k, s_qst, s_raw = S("q_rows"), S("k_rows"), S("q_stored"), S("kv_raw")
        s_tk, s_tz, s_be, s_ze, s_zst = S("kT_psum"), S("zT_psum"), S("kT"), S("zT"), S("z_stored")
        s_gq = S("gain_ready")
        c_act, c_dve, c_pool = S("act_chain"), S("dve_chain"), S("pool_chain")
        c_none = [S("sp_none"), S("pe_none")]
        block = ctx.enter_context(nc.Block())
        x_view = K.x[0].rearrange("(i p) d -> i p d", p=P)
        hT_view = K.hT_d.rearrange("i p k t -> i p (k t)")
        q_view = K.q_d.rearrange("i p n -> i p n")
        zT_view = K.zT_d.rearrange("(c p) t -> p c t", p=P)

        @block.sync
        def _(sp):
            sp.dma_start(xt[:, :], x_view[0]).then_inc(s_x, 16)
            sp.dma_start(gain[:, :], K.attn_norm_g[0].partition_broadcast(P)).then_inc(s_gain, 16)
            for n, g in enumerate((K.q_norm_g[0], K.k_norm_g[0, 1], K.k_norm_g[0, 2])):
                sp.dma_start(gqk1[:, n, :], g.partition_broadcast(P)).then_inc(s_gain, 16)

            def step(j):
                if not (isinstance(j, int) and j == NT - 1):
                    sp.wait_ge(s_h, j + 1)
                    sp.dma_start(xt[:, :], x_view[j + 1]).then_inc(s_x, 16)
                sp.wait_ge(s_hTe, 2 * j + 2)
                sp.dma_start(hT_view[j], hT[:, :, :].rearrange("p k t -> p (k t)")).then_inc(s_hst, 16)
                if not (isinstance(j, int) and j == 0):
                    store_z(j - 1)

            def store_z(j):
                sp.wait_ge(s_ze, j + 2)
                sp.dma_start(zT_view[:, :, ds(HALO + j * P, P)], zT[:, :, :]).then_inc(s_zst, 16)
            sp.sem_inc(s_zst, 16)
            tiles(sp, Chain(sp, c_none[0]), step)
            store_z(NT - 1)
            sp.wait_ge(s_zst, 16 * NT + 16)
            sp.wait_ge(s_hst, 16 * NT)

        @block.gpsimd
        def _(pool):
            c = Chain(pool, c_pool)

            def rsqrt(src, m, dst, inv, sem):
                c.mark(nc.gpsimd.tensor_tensor(m, src, inv[:, 0:dst.shape[1]], ALU.mult))
                c.sync()
                c.mark(nc.gpsimd.tensor_scalar(m, m, EPS, None, ALU.add))
                c.sync()
                nc.gpsimd.tensor_tensor(dst, m, K.mhalf[:, 0:dst.shape[1]], ALU.pow).then_inc(sem, 1)

            def step(j):
                if not (isinstance(j, int) and j == NT - 1):
                    pool.wait_ge(s_ssq, j + 2)
                    rsqrt(ssq[:, :], ms[:, :], rstd[:, :], K.inv_d, s_rstd)
                pool.wait_ge(s_red, j + 1)
                rsqrt(ss12[:, :], ms12[:, :], rr12[:, :], K.inv_hd, s_rr)
                pool.wait_ge(s_q, j + 1)
                pool.dma_start(q_view[j], qrow[:, :, :].rearrange("p h n -> p (h n)")).then_inc(s_qst, 16)
            pool.wait_ge(s_ssq, 1)
            rsqrt(ssq[:, :], ms[:, :], rstd[:, :], K.inv_d, s_rstd)
            tiles(pool, c, step)
            pool.wait_ge(s_qst, 16 * NT)

        @block.scalar
        def _(act):
            c = Chain(act, c_act)

            def squares_x(j):
                act.wait_ge(s_x, 16 * j + 16)
                nc.scalar.activation(junk[:, :], xt[:, :], ACT.Square,
                                     accum_out=ssq[:, :]).then_inc(s_ssq, 1)

            def post(j):
                act.wait_ge(s_tk, j + 1)
                nc.scalar.copy(K.kvT[:, 0, ts(j, P)], B[:, 0, :])
                nc.scalar.copy(K.kvT[:, 1, ts(j, P)], B[:, 1, :])
                for g in range(NKV):
                    rows = slice(g * HD, g * HD + HD)
                    nc.scalar.copy(K.kselT[0:HD, g, ts(j, P)], B[rows, 2, :])
                    last = nc.scalar.copy(K.kwinT[0:HD, g, ds(WINDOW + j * P, P)], B[rows, 3, :])
                last.then_inc(s_be, 1)
                act.wait_ge(s_zst, 16 * j + 16)
                act.wait_ge(s_tz, j + 1)
                nc.scalar.copy(zT[:, :, :], T[0][:, :, :]).then_inc(s_ze, 1)

            def step(j):
                first = isinstance(j, int) and j == 0
                if not first:
                    act.wait_ge(s_hst, 16 * j)
                for n in range(2):
                    act.wait_ge(s_th, 2 * j + n + 1)
                    nc.scalar.copy(hT[:, 4 * n:4 * n + 4, :], T[n][:, :, :]).then_inc(s_hTe, 1)
                if not (isinstance(j, int) and j == NT - 1):
                    squares_x(j + 1)
                if not first:
                    post(j - 1)
                    act.wait_ge(s_red, j)
                act.wait_ge(s_mm, 5 * j + 1)
                nc.scalar.activation(sq[:, 0:NH, :].rearrange("p h n -> p (h n)"), Z[0][:, :], ACT.Square)
                act.wait_ge(s_mm, 5 * j + 2)
                if not first:
                    act.wait_ge(s_tk, j)
                nc.scalar.copy(kvraw[:, :, :].rearrange("p a n -> p (a n)"), Z[1][:, 0:2 * KV_COLS])\
                    .then_inc(s_raw, 1)
                nc.scalar.activation(sq[:, NH:NH + 2, :].rearrange("p h n -> p (h n)"),
                                     Z[1][:, 2 * KV_COLS:3 * KV_COLS], ACT.Square)
                nc.scalar.copy(K.vsel[:, j, :, 0:HD], Z[1][:, 3 * KV_COLS:4 * KV_COLS]
                               .rearrange("p (g n) -> p g n", n=HD))
                act.wait_ge(s_mm, 5 * j + 3)
                nc.scalar.copy(K.vwin[:, WINDOW // P + j, :, 0:HD], Z[2][:, KV_COLS:2 * KV_COLS]
                               .rearrange("p (g n) -> p g n", n=HD))
                nc.scalar.activation(K.gates[:, j, :], Z[2][:, 2 * KV_COLS:2 * KV_COLS + 3 * NH], ACT.Sigmoid)
                nc.scalar.activation(sq[:, NH + 2:NN, :].rearrange("p h n -> p (h n)"),
                                     Z[2][:, 0:KV_COLS], ACT.Square).then_inc(s_sq, 1)
                act.wait_ge(s_mm, 5 * j + 4)
                if not first:
                    act.wait_ge(s_dvez, 4 * j)
                nc.scalar.activation(sg[:, :], Z[3][:, :], ACT.Sigmoid).then_inc(s_actz, 1)
            act.sem_inc(s_ze, 1)
            act.sem_inc(s_be, 1)
            squares_x(0)
            tiles(act, c, step)
            post(NT - 1)

        @block.vector
        def _(dve):
            c = Chain(dve, c_dve)
            dve.wait_ge(s_gain, 64)
            c.mark(nc.vector.tensor_scalar(gqk[:, 0:NH, :], gqk1[:, 0:1, :].to_broadcast([P, NH, HD]),
                                           SCALE, None, ALU.mult))
            for n in range(2):
                c.mark(nc.vector.tensor_copy(gqk[:, NH + 2 * n:NH + 2 * n + 2, :],
                                             gqk1[:, n + 1:n + 2, :].to_broadcast([P, 2, HD])))
            for h_ in range(NH):
                c.mark(nc.vector.memset(qrow[:, h_, HD:HD + 1], 2.0 ** (-8.0 * (h_ + 1) / NH)))
            c.sync()

            def norm_x():
                nc.vector.scalar_tensor_tensor(h[:, :], xt[:, :], rstd[:, 0:1], gain[:, :],
                                               ALU.mult, ALU.mult).then_inc(s_h, 1)

            def head_scale(dst, src, a, b):
                return nc.vector.tensor_tensor(nrm[:, a:b, :], src.rearrange("p (h n) -> p h n", n=HD),
                                               rr12[:, a:b].unsqueeze(2).to_broadcast([P, b - a, HD]), ALU.mult)

            def step(j):
                first = isinstance(j, int) and j == 0
                if not (isinstance(j, int) and j == NT - 1):
                    dve.wait_ge(s_rstd, j + 2)
                    dve.wait_ge(s_th, 2 * j + 2)
                    norm_x()
                dve.wait_ge(s_sq, j + 1)
                nc.vector.tensor_reduce(ss12[:, :], sq[:, :, :], AX, ALU.add).then_inc(s_red, 1)
                dve.wait_ge(s_rr, j + 1)
                head_scale(nrm, Z[0][:, :], 0, NH).then_inc(s_dvez, 1)
                head_scale(nrm, Z[1][:, 2 * KV_COLS:3 * KV_COLS], NH, NH + 2).then_inc(s_dvez, 1)
                head_scale(nrm, Z[2][:, 0:KV_COLS], NH + 2, NN).then_inc(s_dvez, 1)
                if not first:
                    dve.wait_ge(s_qst, 16 * j)
                nc.vector.tensor_scalar(qrow[:, :, HD + 1], K.nslope[:, :], K.tpos[:, ds(j, 1)], None, ALU.mult)
                dve.wait_ge(s_dvez, 4 * j + 3)
                nc.vector.tensor_tensor(qrow[:, :, 0:HD], nrm[:, 0:NH, :], gqk[:, 0:NH, :],
                                        ALU.mult).then_inc(s_q, 1)
                if not first:
                    dve.wait_ge(s_tk, j)
                nc.vector.tensor_tensor(krow[:, :, :].rearrange("p a (g n) -> p (a g) n", n=HD),
                                        nrm[:, NH:NN, :], gqk[:, NH:NN, :], ALU.mult).then_inc(s_k, 1)
                dve.wait_ge(s_actz, j + 1)
                dve.wait_ge(s_mm, 5 * j + 5)
                if not first:
                    dve.wait_ge(s_tz, j)
                nc.vector.tensor_tensor(zrow[:, :], Z[4][:, :], sg[:, :], ALU.mult).then_inc(s_dvez, 1)
            dve.wait_ge(s_rstd, 1)
            norm_x()
            tiles(dve, c, step)

        @block.tensor
        def _(pe):
            def post(j):
                pe.wait_ge(s_be, j + 1)
                pe.wait_ge(s_raw, j + 1)
                pe.wait_ge(s_k, j + 1)
                for n in range(4):
                    src = kvraw[:, n, :] if n < 2 else krow[:, n - 2, :]
                    last = nc.tensor.transpose(B[:, n, :], src, K.ident[:, :])
                last.then_inc(s_tk, 1)
                pe.wait_ge(s_dvez, 4 * j + 4)
                if not (isinstance(j, int) and j == NT - 1):
                    pe.wait_ge(s_hTe, 2 * j + 3)
                for n in range(NCH):
                    last = nc.tensor.transpose(T[0][:, n, :], zrow[:, ts(n, P)], K.ident[:, :])
                last.then_inc(s_tz, 1)

            def step(j):
                first = isinstance(j, int) and j == 0
                pe.wait_ge(s_h, j + 1)
                if not first:
                    pe.wait_ge(s_ze, j)
                for n in range(2):
                    for k in range(4):
                        last = nc.tensor.transpose(T[n][:, k, :], h[:, ts(4 * n + k, P)], K.ident[:, :])
                    last.then_inc(s_th, 1)
                if not first:
                    post(j - 1)
                pe.wait_ge(s_hTe, 2 * j + 2)
                for n, (o, m) in enumerate(CHUNKS):
                    if first:
                        pe.wait_ge(s_w[n], 16)
                    else:
                        if n == 3:
                            pe.wait_ge(s_actz, j)
                        else:
                            pe.wait_ge(s_dvez, 4 * (j - 1) + min(n, 3) + 1)
                    for k in range(KD):
                        last = nc.tensor.matmul(Z[n][:, 0:m], hT[:, k, :], w[:, k, o:o + m],
                                                start=(k == 0), stop=(k == KD - 1))
                    last.then_inc(s_mm, 1)
            tiles(pe, Chain(pe, c_none[1]), step)
            post(NT - 1)


def compress(nc, K):
    with ExitStack() as ctx:
        sb, ps = bufs(nc, ctx, "c_")
        w1 = sb("w1", [P, 2, CMP_BLOCK, CMP_HID])
        w2 = sb("w2", [P, 2, HD])
        pos, posT = sb("pos", [CMP_BLOCK, 2, HD]), sb("posT", [HD, 2, CMP_BLOCK])
        bias = sb("bias", [P, 2])
        hid = sb("hid", [P, 4, P])
        gain = sb("gain_c", [P, HD])
        sq, nrm, row = sb("sq_c", [P, NKV, HD]), sb("nrm_c", [P, NKV, HD]), sb("row_c", [P, NKV, HD])
        ss, ms, rr = sb("ss_c", [P, NKV]), sb("ms_c", [P, NKV]), sb("rr_c", [P, NKV])
        H = [ps(f"H{i}", [P, 512]) for i in range(4)]
        PB = [ps(f"PB{i}", [P, 512]) for i in range(2)]
        O, T = ps("Oc", [P, 4, HD]), ps("Tc", [P, 512])
        S = Sems(nc, ctx, "c")
        s_w = [S("w1k"), S("w1v")]
        s_l, s_pt, s_pe, s_b, s_bs = S("loads"), S("posT_psum"), S("posT"), S("bias_psum"), S("bias")
        s_h, s_g, s_o, s_sq, s_ss, s_rr, s_row = (S("hid_psum"), S("hid"), S("out"), S("sq"), S("ss"), S("rr"),
                                                  S("row"))
        s_t, s_p = S("kT"), S("pool_chain")
        s_n, s_mk = S("nrm"), S("mask_chain")
        block = ctx.enter_context(nc.Block())

        @block.sync
        def _(sp):
            for a in range(2):
                sp.dma_start(pos[:, a, :], K.cmp_pos[0, a]).then_inc(s_l, 16)
                sp.dma_start(w2[:, a, :], K.cmp_w2[0, a]).then_inc(s_l, 16)
            sp.dma_start(gain[:, :], K.k_norm_g[0, 0].partition_broadcast(P)).then_inc(s_l, 16)
            for a in range(2):
                src = K.cmp_w1[0, a].rearrange("(l d) h -> d l h", d=HD)
                for g in range(NKV):
                    sp.dma_start(w1[g * HD:g * HD + HD, a, :, :], src).then_inc(s_w[a], 16)

        @block.tensor
        def _(pe):
            pe.wait_ge(s_l, 80)
            for a in range(2):
                last = nc.tensor.transpose(T[0:HD, a * CMP_BLOCK:(a + 1) * CMP_BLOCK], pos[:, a, :],
                                           K.ident[0:CMP_BLOCK, 0:CMP_BLOCK])
            last.then_inc(s_pt, 1)
            for a in range(2):
                pe.wait_ge(s_w[a], 32)
                for g in range(NKV):
                    rows = slice(g * HD, g * HD + HD)
                    for l in range(CMP_BLOCK):
                        last = nc.tensor.matmul(H[2 * a + g][:, 0:NC], w1[rows, a, l, :],
                                                K.kvT[rows, a, l:l + CMP_STRIDE * (NC - 1) + 1:CMP_STRIDE],
                                                start=(l == 0), stop=(l == CMP_BLOCK - 1))
                last.then_inc(s_h, 1)
                if a == 0:
                    pe.wait_ge(s_pe, 1)
                for l in range(CMP_BLOCK):
                    last = nc.tensor.matmul(PB[a][:, 0:1], w1[0:HD, a, l, :], posT[:, a, l:l + 1],
                                            start=(l == 0), stop=(l == CMP_BLOCK - 1))
                last.then_inc(s_b, 1)
            for a in range(2):
                pe.wait_ge(s_g, a + 1)
                for g in range(NKV):
                    last = nc.tensor.matmul(O[0:NC, 2 * a + g, :], hid[:, 2 * a + g, 0:NC], w2[:, a, :],
                                            start=True, stop=True)
                last.then_inc(s_o, 1)
            pe.wait_ge(s_row, 1)
            nc.tensor.transpose(T[:, 0:NC], row[0:NC, :, :].rearrange("p g n -> p (g n)"),
                                K.ident[0:NC, 0:NC]).then_inc(s_t, 1)

        @block.scalar
        def _(act):
            act.wait_ge(s_pt, 1)
            nc.scalar.copy(posT[:, :, :].rearrange("p a l -> p (a l)"), T[0:HD, 0:2 * CMP_BLOCK])\
                .then_inc(s_pe, 1)
            for a in range(2):
                act.wait_ge(s_b, a + 1)
                nc.scalar.copy(bias[:, a:a + 1], PB[a][:, 0:1]).then_inc(s_bs, 1)
                act.wait_ge(s_bs, a + 1)
                for g in range(NKV):
                    last = nc.scalar.activation(hid[:, 2 * a + g, 0:NC], H[2 * a + g][:, 0:NC],
                                                ACT.Gelu_apprx_tanh, bias=bias[:, a:a + 1])
                last.then_inc(s_g, 1)
            act.wait_ge(s_o, 2)
            nc.scalar.copy(K.vc[0:NC, :, :], O[0:NC, 2:4, :])
            nc.scalar.activation(sq[0:NC, :, :], O[0:NC, 0:2, :], ACT.Square).then_inc(s_sq, 1)
            act.wait_ge(s_t, 1)
            for g in range(NKV):
                nc.scalar.copy(K.kcT[0:HD, g, 0:NC], T[g * HD:g * HD + HD, 0:NC])

        @block.vector
        def _(dve):
            dve.wait_ge(s_sq, 1)
            nc.vector.tensor_reduce(ss[0:NC, :], sq[0:NC, :, :], AX, ALU.add).then_inc(s_ss, 1)
            dve.wait_ge(s_rr, 1)
            nc.vector.tensor_tensor(nrm[0:NC, :, :], O[0:NC, 0:2, :],
                                    rr[0:NC, :].unsqueeze(2).to_broadcast([NC, NKV, HD]),
                                    ALU.mult).then_inc(s_n, 1)
            dve.wait_ge(s_n, 1)
            dve.wait_ge(s_l, 80)
            nc.vector.tensor_tensor(row[0:NC, :, :], nrm[0:NC, :, :],
                                    gain[0:NC, :].unsqueeze(1).to_broadcast([NC, NKV, HD]),
                                    ALU.mult).then_inc(s_row, 1)

        @block.gpsimd
        def _(pool):
            c = Chain(pool, s_mk)

            def put(ins):
                c.mark(ins)
                c.sync()
            make_masks(nc, K, put)
            pool.wait_ge(s_ss, 1)
            nc.gpsimd.tensor_scalar(ms[0:NC, :], ss[0:NC, :], 1.0 / HD, EPS, ALU.mult, ALU.add).then_inc(s_p, 1)
            pool.wait_ge(s_p, 1)
            nc.gpsimd.tensor_tensor(rr[0:NC, :], ms[0:NC, :], K.mhalf[0:NC, 0:NKV], ALU.pow).then_inc(s_rr, 1)


def load_merge_weights(eng, K, half):
    for b in range(2):
        o = OFF_MERGE + b * D + half * (D // 2)
        eng.dma_start(K.wm[half][:, :, ts(b, D // 2)],
                      K.w_in[0].rearrange("(k p) n -> p k n", p=P)[:, :, o:o + D // 2]).then_inc(K.s_wm, 16)


def split_keys(nc, K):
    with ExitStack() as ctx:
        S = Sems(nc, ctx, "s")
        s_b, s_a, s_z = S("high"), S("done"), S("zeroed")
        block = ctx.enter_context(nc.Block())

        @block.scalar
        def _(act):
            for g in range(NKV):
                nc.scalar.copy(K.keyB[:, g, :], K.kselT[:, g, :]).then_inc(s_b, 1)
            act.wait_ge(s_b, 2)
            for g in range(NKV):
                nc.scalar.copy(K.keyA[0:HD, g, :], K.keyB[0:HD, g, :].bitcast(F32))

        @block.sync
        def _(sp):
            load_merge_weights(sp, K, 0)
            sp.wait_ge(s_z, 1)
            sp.dma_start(K.y_d[NE * P:, :].rearrange("(b p) n -> p b n", p=P),
                         K.zero_row[:, :].unsqueeze(1).to_broadcast([P, MAX_BLK - NE, D])).then_inc(K.s_zero, 16)

        @block.vector
        def _(dve):
            nc.vector.memset(K.zero_row[:, :], 0.0).then_inc(s_z, 1)
            for g in range(NKV):
                dve.wait_ge(s_b, g + 1)
                nc.vector.tensor_tensor(K.keyA[HD:P, g, :], K.kselT[0:HD, g, :],
                                        K.keyB[0:HD, g, :].bitcast(F32), ALU.subtract).then_inc(s_a, 1)


def attention_plan(W):
    def mix(a, b):
        out, n = [], 0
        for k, x in enumerate(a):
            out.append(x)
            upto = (k + 1) * len(b) // len(a)
            out += b[n:upto]
            n = upto
        return out
    wm = [[("Mw", h) for h in range(g * HPG, g * HPG + HPG)] + [("Mt", g)] for g in range(NKV)]
    ws = [[("Sw", g, c) for c in range(5)] for g in range(NKV)]
    sm = [[("Ms", h, s) for h in range(g * HPG, g * HPG + HPG) for s in range(W)] for g in range(NKV)]
    ss = [[("Ss", g, c) for c in range(4 * W)] for g in range(NKV)]
    seq = [("Q", 0), ("Q", 1), ("low", 0), ("low", 1)] + wm[0] + [("fin", 0, 0), ("Xm", 0, 0), ("C", 0), ("C", 1)]
    seq += ws[0][:2] + [("norm", 0), ("norm", 1)] + ws[0][2:] + [("Xc", 0), ("Xc", 1), ("cv",), ("blocks",)]
    seq += wm[1] + [("fin", 0, 1), ("Xm", 0, 1), ("Xb",)] + mix(sm[0], ws[1])
    seq += [("fin", 1, 0), ("Xm", 1, 0), ("used", 0, 0), ("used", 0, 1)]
    seq += mix(sm[1], ss[0]) + [("fin", 1, 1), ("Xm", 1, 1), ("used", 1, 0)] + ss[1] + [("used", 1, 1), ("Xo",)]
    out, pend, group = [], [], None
    for st in seq:
        if st[0] in ("Sw", "Ss"):
            out.append(st)
            pend.append(st)
            if len(pend) > 2:
                out.append(("pv",) + pend.pop(0))
        elif st[0] in ("used", "Xo"):
            while pend and (st[0] == "Xo" or (pend[0][0], pend[0][1]) == (("Sw", "Ss")[st[1]], st[2])):
                out.append(("pv",) + pend.pop(0))
            out.append(st)
        else:
            out.append(st)
    return out


def attend(nc, K, quarter):
    W = quarter + 1
    TQ = NT // 4
    plan = attention_plan(W)
    JOBS = [st for st in plan if st[0][0] in "QCMSX"]
    ON_DVE = [st[0] in ("Mw", "Mt", "Ms") for st in JOBS]
    job_of = {st: n for n, st in enumerate(JOBS)}
    PVS = [st[1:] for st in plan if st[0] == "pv"]
    EXPS = [st for st in JOBS if st[0] in ("Sw", "Ss")]
    assert EXPS == PVS and len(JOBS) % 4 == 0
    NJ, NV = len(JOBS), len(PVS)
    ND = sum(ON_DVE)
    NA = NJ - ND
    RING = 4
    with ExitStack() as ctx:
        sb, ps = bufs(nc, ctx, f"b{quarter}_")
        qrow = sb("q_tile", [P, NH, AUG])
        qT = sb("qT", [AUG, NH, P])
        qM = sb("q_high", [P, NH, P], F32R)
        qA = sb("q_high_twice", [P, NH, P], F32R)
        qBw = sb("q_low_win", [67, NH, P], F32R)
        qBs = sb("q_low_sel", [P, NH, P], F32R)
        wA, wB = sb("keyA_win", [P, NKV, 5 * P], F32R), sb("keyB_win", [67, NKV, 5 * P], F32R)
        aug = sb("q_extra", [P, 2, NH, 3])
        Pc, Pn, PcT = sb("p_cmp", [P, NH, P]), sb("p_cmp_n", [P, NH, P]), sb("p_cmpT", [P, NH, P])
        PT = sb("pT_ring", [P, RING, HPG * P])
        nmc, smc, rc = sb("nmax_c", [P, NH]), sb("sum_c", [P, NH]), sb("rcp_c", [P, NH])
        pcs = sb("p_head_sum", [P, NKV, P])
        imp, imp2 = sb("imp", [P, NKV, NSB]), sb("imp2", [P, NKV, NSB])
        top = sb("top", [P, NKV, 8])
        rep, pen = sb("replaced", [P, NKV, NSB]), sb("unselected", [P, NKV, NSB])
        mx = [sb("max_win", [P, NH, 2]), sb("max_sel", [P, NH, W])]
        rcp, fac = sb("rcp_head", [P, HPG]), sb("gate_over_sum", [P, HPG])
        o, op = sb("o_rows", [P, NH, HD]), sb("o_part", [P, HPG, HD])
        oT = sb("oT", [P, KF, P])
        X = [ps(f"X{i}", [P, 4, P]) for i in range(4)]
        O = [[ps(f"O{b}{g}", [P, 512]) for g in range(NKV)] for b in range(2)]
        S = Sems(nc, ctx, f"b{quarter}")
        s_q, s_z, s_fill, s_fA, s_fD = S("q_loaded"), S("zeroed"), S("filled"), S("read_act"), S("read_dve")
        s_cm, s_pn, s_low, s_mx = S("cmp_max"), S("cmp_probs"), S("q_low"), S("minus_max")
        s_wk, s_qa = S("win_keys"), S("q_parts")
        s_pen, s_cv, s_cc, s_pv, s_use = S("unselected"), S("cmp_out"), S("cmp_used"), S("values"), S("used")
        s_oa, s_ost = S("o_rows"), S("o_stored")
        c_dve, c_act, c_pool, c_x = S("dve_chain"), S("act_chain"), S("pool_chain"), [S("none0"), S("none1")]
        block = ctx.enter_context(nc.Block())

        def each_tile(eng, chain, body):
            with eng.Fori(0, TQ) as it:
                body(it)
                chain.restart()

        def bank(st):
            return X[job_of[st] % 4]

        def filled(eng, it, st):
            eng.wait_ge(s_fill, it * NJ + job_of[st] + 1)

        def read(eng, it, st):
            n = job_of[st]
            if ON_DVE[n]:
                eng.wait_ge(s_fD, it * ND + sum(ON_DVE[:n + 1]))
            else:
                eng.wait_ge(s_fA, it * NA + n + 2 - sum(ON_DVE[:n + 1]))

        @block.sync
        def _(sp):
            def load(i):
                sp.dma_start(qrow[:, :, :].rearrange("p h n -> p (h n)"), K.q_d[i]).then_inc(s_q, 16)
            load(quarter * TQ)
            with sp.Fori(1, TQ) as it:
                sp.wait_ge(s_mx, it * 4)
                load(quarter * TQ + it)
            if quarter == 3:
                sp.wait_ge(K.s_zero, 16)

        @block.gpsimd
        def _(pool):
            c = Chain(pool, c_pool)
            pool.sem_inc(s_use, 1)

            def put(ins):
                c.mark(ins)
                c.sync()
            put(nc.gpsimd.memset(qM[HD:P, :, :].bitcast(F32), 0.0))
            nc.gpsimd.memset(qBs[HD:P, :, :].bitcast(F32), 0.0).then_inc(s_z, 1)
            pool.wait_ge(s_z, 1)
            c.restart()

            def body(it):
                i = quarter * TQ + it
                pool.wait_ge(s_use, it + 1)
                keys = K.kwinT[0:67, :, ds(i * P, 5 * P)]
                put(nc.gpsimd.tensor_copy(wB[:, :, :], keys))
                put(nc.gpsimd.tensor_copy(wA[0:HD, :, :], wB[0:HD, :, :].bitcast(F32)))
                nc.gpsimd.tensor_tensor(wA[HD:P, :, :], K.kwinT[0:HD, :, ds(i * P, 5 * P)],
                                        wB[0:HD, :, :].bitcast(F32), ALU.subtract).then_inc(s_wk, 1)
                pool.wait_ge(s_wk, it + 1)
                for g in range(NKV):
                    heads = slice(g * HPG, (g + 1) * HPG)
                    read(pool, it, ("Q", g))
                    high = qM[0:HD, heads, :].bitcast(F32)
                    put(nc.gpsimd.tensor_tensor(qBs[0:HD, heads, :], qT[0:HD, heads, :], high, ALU.subtract))
                    put(nc.gpsimd.tensor_copy(qA[0:HD, heads, :], high))
                    nc.gpsimd.tensor_copy(qA[HD:P, heads, :], high).then_inc(s_qa, 1)
                    pool.wait_ge(s_qa, it * 2 + g + 1)
                    pool.sem_inc(c_pool, 1)
                    c.n += 1
                    c.sync()
            each_tile(pool, c, body)

        @block.tensor
        def _(pe):
            def wide(mask):
                return mask.unsqueeze(1).to_broadcast([P, HPG, P])

            def fill(it, i, st):
                kind = st[0]
                n = job_of[st]
                if n >= 4:
                    read(pe, it, JOBS[n - 4])
                b = bank(st)
                flat = b[:, :, :].rearrange("p c k -> p (c k)")
                if kind == "Q":
                    g = st[1]
                    for r in range(HPG):
                        last = nc.tensor.transpose(b[0:AUG, r, :], qrow[:, g * HPG + r, :], K.ident[:, :])
                elif kind == "C":
                    g = st[1]
                    read(pe, it, ("Q", g))
                    for r in range(HPG):
                        nc.tensor.matmul(b[:, r, :], qT[:, g * HPG + r, :], K.kcT[0:AUG, g, :],
                                         start=True, stop=False)
                        last = nc.tensor.matmul(b[:, r, :], K.identb[:, :], K.m_cmp[:, ds(NEGC - 8 * i, P)],
                                                start=False, stop=True)
                elif kind == "Mw":
                    h = st[1]
                    if h == 0:
                        pe.wait_ge(s_wk, it + 1)
                    if h % HPG == 0:
                        read(pe, it, ("Q", h // HPG))
                    nc.tensor.matmul(flat, qM[0:AUG, h, :], wB[0:AUG, h // HPG, 0:QB], start=True, stop=False)
                    last = nc.tensor.matmul(flat[:, 0:P], K.identb[:, :], K.m_old[:, :], start=False, stop=True)
                elif kind == "Mt":
                    for r in range(HPG):
                        nc.tensor.matmul(b[:, r, :], qM[0:AUG, st[1] * HPG + r, :], wB[0:AUG, st[1], QB:5 * P],
                                         start=True, stop=False)
                        last = nc.tensor.matmul(b[:, r, :], K.identb[:, :], K.m_causal[:, QB - P:QB],
                                                start=False, stop=True)
                elif kind == "Ms":
                    h, s = st[1:]
                    tail = s == W - 1
                    if (h, s) == (0, 0):
                        read(pe, it, ("Xb",))
                    last = nc.tensor.matmul(flat, qM[:, h, :], K.keyB[:, h // HPG, ts(s, QB)],
                                            start=True, stop=not tail)
                    if tail:
                        last = nc.tensor.matmul(flat, K.identb[:, :], K.m_causal[:, ds(QB - P - it * P, QB)],
                                                start=False, stop=True)
                elif kind == "Xc":
                    g = st[1]
                    pe.wait_ge(s_pn, it * 2 + g + 1)
                    for r in range(HPG):
                        last = nc.tensor.transpose(b[:, r, :], Pn[:, g * HPG + r, :], K.ident[:, :])
                elif kind == "Xm":
                    br, g = st[1:]
                    pe.wait_ge(s_mx, it * 4 + br * 2 + g + 1)
                    for r in range(HPG):
                        last = nc.tensor.transpose(b[0:3, r, :], aug[:, br, g * HPG + r, :], K.ident[:, :])
                elif kind == "Xb":
                    pe.wait_ge(s_pen, it + 1)
                    for g in range(NKV):
                        last = nc.tensor.transpose(b[0:NSB, g, :], pen[:, g, :], K.ident[:, :])
                elif kind == "Xo":
                    pe.wait_ge(s_oa, it + 1)
                    orow = o[:, :, :].rearrange("p h n -> p (h n)")
                    for k in range(KF):
                        last = nc.tensor.transpose(b[:, k, :], orow[:, ts(k, P)], K.ident[:, :])
                elif kind == "Sw":
                    g, c = st[1:]
                    heads = slice(g * HPG, (g + 1) * HPG)
                    if c == 0:
                        read(pe, it, ("Xm", 0, g))
                        pe.wait_ge(s_low, it * 2 + g + 1)
                        pe.wait_ge(s_qa, it * 2 + g + 1)
                    edge = c in (0, 4)
                    nc.tensor.matmul(b[:, :, :], wA[:, g, ts(c, P)], qA[:, heads, :], start=True, stop=False)
                    last = nc.tensor.matmul(b[:, :, :], wB[:, g, ts(c, P)], qBw[:, heads, :],
                                            start=False, stop=not edge)
                    if edge:
                        mask = K.mT_old[:, :] if c == 0 else K.mT_causal[:, QB - P:QB]
                        last = nc.tensor.matmul(b[:, :, :], K.identb[:, :], wide(mask), start=False, stop=True)
                else:
                    g, c = st[1:]
                    heads = slice(g * HPG, (g + 1) * HPG)
                    if c == 0:
                        read(pe, it, ("Xm", 1, g))
                        read(pe, it, ("Xb",))
                    own = c - 4 * (W - 1)
                    nc.tensor.matmul(b[:, :, :], K.keyA[:, g, ts(c, P)], qA[:, heads, :], start=True, stop=False)
                    last = nc.tensor.matmul(b[:, :, :], K.keyB[:, g, ts(c, P)], qBs[:, heads, :],
                                            start=False, stop=own < 0)
                    if own >= 0:
                        mask = K.mT_causal[:, ds(QB - P - own * P + it * P, P)]
                        last = nc.tensor.matmul(b[:, :, :], K.identb[:, :], wide(mask), start=False, stop=True)
                last.then_inc(s_fill, 1)

            def values(it, i, st):
                kind, g, c = st
                read(pe, it, st)
                br = ("Sw", "Ss").index(kind)
                if st == ("Ss", 0, 0):
                    pe.wait_ge(s_cc, it + 1)
                v = K.vsel[:, c, g, :] if br else K.vwin[:, ds(i + c, 1), g, :].rearrange("p a n -> p (a n)")
                for r in range(HPG):
                    last = nc.tensor.matmul(O[br][g][:, r * (HD + 1):(r + 1) * (HD + 1)],
                                            PT[:, EXPS.index(st) % RING, ts(r, P)], v,
                                            start=(c == 0 and r == 0), stop=(c == (4, 4 * W - 1)[br] and r == HPG - 1))
                last.then_inc(s_pv, 1)

            def body(it):
                i = quarter * TQ + it
                pe.wait_ge(s_q, it * 16 + 16)
                pe.wait_ge(s_fA, it * NA + 1)
                for st in plan:
                    if st in job_of:
                        fill(it, i, st)
                    elif st[0] == "pv":
                        values(it, i, st[1:])
                    elif st[0] == "cv":
                        for h in range(NH):
                            read(pe, it, ("Xc", h // HPG))
                            last = nc.tensor.matmul(O[1][0][:, ts(h, HD)], PcT[:, h, :], K.vc[:, h // HPG, :],
                                                    start=True, stop=True)
                        last.then_inc(s_cv, 1)
            pe.wait_ge(s_z, 1)
            each_tile(pe, Chain(pe, c_x[0]), body)

        @block.scalar
        def _(act):
            c = Chain(act, c_act)

            def body(it):
                for st in JOBS:
                    kind = st[0]
                    if ON_DVE[job_of[st]]:
                        continue
                    b = bank(st)
                    if kind != "C":
                        filled(act, it, st)
                    if kind == "Q":
                        heads = slice(st[1] * HPG, (st[1] + 1) * HPG)
                        nc.scalar.copy(qM[0:AUG, heads, :], b[0:AUG, :, :])
                        last = nc.scalar.copy(qT[:, heads, :], b[0:AUG, :, :])
                    elif kind == "C":
                        act.wait_ge(s_cm, it * 2 + st[1] + 1)
                        for r in range(HPG):
                            h = st[1] * HPG + r
                            last = nc.scalar.activation(Pc[:, h, :], b[:, r, :], ACT.Exp,
                                                        bias=nmc[:, h:h + 1], accum_out=smc[:, h:h + 1])
                    elif kind == "Xc":
                        last = nc.scalar.copy(PcT[:, st[1] * HPG:(st[1] + 1) * HPG, :], b[:, :, :])
                    elif kind == "Xm":
                        to = (qBw, qBs)[st[1]]
                        last = nc.scalar.copy(to[HD:67, st[2] * HPG:(st[2] + 1) * HPG, :], b[0:3, :, :])
                    elif kind == "Xb":
                        for g in range(NKV):
                            src = b[0:NSB, g:g + 1, :].to_broadcast([NSB, HPG, P])
                            nc.scalar.copy(qM[96:P, g * HPG:(g + 1) * HPG, :], src)
                            last = nc.scalar.copy(qBs[96:P, g * HPG:(g + 1) * HPG, :], src)
                    elif kind == "Xo":
                        act.wait_ge(s_ost, it * 16 + 16)
                        last = nc.scalar.copy(oT[:, :, :], b[:, :, :])
                    else:
                        k = EXPS.index(st)
                        if k >= RING:
                            act.wait_ge(s_pv, it * NV + k - RING + 1)
                        last = nc.scalar.activation(PT[:, k % RING, :], b[:, :, :].rearrange("p c k -> p (c k)"),
                                                    ACT.Exp)
                    last.then_inc(s_fA, 1)
                read(act, it, ("Xo",))
                act.dma_start(K.oT_d[quarter * TQ + it].rearrange("p k t -> p (k t)"),
                              oT[:, :, :].rearrange("p k t -> p (k t)")).then_inc(s_ost, 16)
            act.sem_inc(s_fA, 1)
            act.sem_inc(s_ost, 16)
            each_tile(act, c, body)
            act.wait_ge(s_ost, 16 * TQ + 16)

        @block.vector
        def _(dve):
            c = Chain(dve, c_dve)

            def put(ins):
                c.mark(ins)
                c.sync()

            def choose(it, i):
                dve.wait_ge(s_pn, it * 2 + 2)
                for g in range(NKV):
                    c.mark(nc.vector.tensor_reduce(pcs[:, g, :], Pn[:, g * HPG:(g + 1) * HPG, :]
                                                   .rearrange("p r n -> p n r"), AX, ALU.add))
                c.sync()
                put(nc.vector.tensor_reduce(imp[:, :, :], pcs[:, :, :].rearrange("p g (j n) -> p g j n", n=4),
                                            AX, ALU.add))
                for g in range(NKV):
                    c.mark(nc.vector.tensor_tensor(imp[:, g, 1:NSB], imp[:, g, 1:NSB],
                                                   pcs[:, g, 3:P - 1:4], ALU.add))
                c.sync()
                for g in range(NKV):
                    c.mark(nc.vector.tensor_tensor(imp2[:, g, :], imp[:, g, :],
                                                   K.forced[:, ds(NSB - 2 - 2 * i, NSB)], ALU.max))
                c.sync()
                for g in range(NKV):
                    c.mark(nc.vector.tensor_tensor(imp[:, g, :], imp2[:, g, :],
                                                   K.valid[:, ds(NSB - 2 - 2 * i, NSB)], ALU.min))
                c.sync()
                put(nc.vector.memset(imp[:, :, 0:1], BIG))
                for g in range(NKV):
                    c.mark(nc.vector.max(top[:, g, :], imp[:, g, :]))
                c.sync()
                for g in range(NKV):
                    c.mark(nc.vector.match_replace(rep[:, g, :], top[:, g, :], imp[:, g, :], -3 * BIG))
                c.sync()
                nc.vector.tensor_tensor(pen[:, :, :], rep[:, :, :], imp[:, :, :], ALU.is_equal).then_inc(s_pen, 1)

            def use(it, i, br, g):
                last_pv = max(k for k, st in enumerate(PVS) if st[0:2] == (("Sw", "Ss")[br], g))
                dve.wait_ge(s_pv, it * NV + last_pv + 1)
                rows = O[br][g][:, 0:HPG * (HD + 1)].rearrange("p (h n) -> p h n", n=HD + 1)
                heads = slice(g * HPG, (g + 1) * HPG)
                put(nc.vector.reciprocal(rcp[:, :], rows[:, :, HD]))
                gate = K.gates[:, ds(i, 1), 3 * g * HPG + (2, 1)[br]:3 * (g + 1) * HPG:3]\
                    .rearrange("p a h -> p (a h)")
                put(nc.vector.tensor_tensor(fac[:, :], rcp[:, :], gate, ALU.mult))
                put(nc.vector.tensor_tensor(op[:, :, :], rows[:, :, 0:HD], fac[:, :].unsqueeze(2)
                                            .to_broadcast([P, HPG, HD]), ALU.mult))
                if (br, g) == (0, 0):
                    dve.wait_ge(s_cc, it + 1)
                last = nc.vector.tensor_tensor(o[:, heads, :], o[:, heads, :], op[:, :, :], ALU.add)
                if g == 0:
                    put(last)
                else:
                    last.then_inc((s_use, s_oa)[br], 1)

            def body(it):
                i = quarter * TQ + it
                for st in plan:
                    kind = st[0]
                    if kind == "C":
                        filled(dve, it, st)
                        nc.vector.tensor_reduce(nmc[:, st[1] * HPG:(st[1] + 1) * HPG], bank(st)[:, :, :], AX,
                                                ALU.max, negate=True).then_inc(s_cm, 1)
                    elif kind == "low":
                        heads = slice(st[1] * HPG, (st[1] + 1) * HPG)
                        if st[1] == 0:
                            dve.wait_ge(s_q, it * 16 + 16)
                            for br in range(2):
                                c.mark(nc.vector.tensor_copy(aug[:, br, :, 0:2], qrow[:, :, HD:AUG]))
                        read(dve, it, ("Q", st[1]))
                        nc.vector.tensor_tensor(qBw[0:HD, heads, :], qT[0:HD, heads, :],
                                                qM[0:HD, heads, :].bitcast(F32), ALU.subtract).then_inc(s_low, 1)
                    elif kind == "norm":
                        heads = slice(st[1] * HPG, (st[1] + 1) * HPG)
                        read(dve, it, ("C", st[1]))
                        put(nc.vector.reciprocal(rc[:, heads], smc[:, heads]))
                        put(nc.vector.tensor_scalar(rc[:, heads], rc[:, heads], K.has_cmp[:, ds(i, 1)], None,
                                                    ALU.mult))
                        nc.vector.tensor_tensor(Pn[:, heads, :], Pc[:, heads, :],
                                                rc[:, heads].unsqueeze(2).to_broadcast([P, HPG, P]), ALU.mult)\
                            .then_inc(s_pn, 1)
                    elif kind in ("Mw", "Ms"):
                        filled(dve, it, st)
                        br = ("Mw", "Ms").index(kind)
                        s = st[2] if br else 0
                        nc.vector.tensor_reduce(mx[br][:, st[1], s:s + 1],
                                                bank(st)[:, :, :].rearrange("p c k -> p (c k)"), AX,
                                                ALU.max).then_inc(s_fD, 1)
                    elif kind == "Mt":
                        filled(dve, it, st)
                        nc.vector.tensor_reduce(mx[0][:, st[1] * HPG:(st[1] + 1) * HPG, 1], bank(st)[:, :, :], AX,
                                                ALU.max).then_inc(s_fD, 1)
                    elif kind == "fin":
                        br, g = st[1:]
                        heads = slice(g * HPG, (g + 1) * HPG)
                        tail = ("Mt", g) if br == 0 else ("Ms", (g + 1) * HPG - 1, W - 1)
                        read(dve, it, tail)
                        nc.vector.tensor_reduce(aug[:, br, heads, 2], mx[br][:, heads, :], AX, ALU.max,
                                                negate=True).then_inc(s_mx, 1)
                    elif kind == "blocks":
                        choose(it, i)
                        dve.wait_ge(s_cv, it + 1)
                        gate = K.gates[:, ds(i, 1), 0:3 * NH:3].rearrange("p a h -> p (a h)")\
                            .unsqueeze(2).to_broadcast([P, NH, HD])
                        nc.vector.tensor_tensor(o[:, :, :], O[1][0][:, :].rearrange("p (h n) -> p h n", n=HD),
                                                gate, ALU.mult).then_inc(s_cc, 1)
                    elif kind == "used":
                        use(it, i, st[1], st[2])
            each_tile(dve, c, body)


def wait_if(eng, sem, v):
    if not isinstance(v, int) or v > 0:
        eng.wait_ge(sem, v)


def lagged(eng, chain, step):
    step(0, True, False, False)
    step(1, True, True, False)
    chain.restart()
    with eng.Fori(2, NT) as j:
        step(j, True, True, True)
        chain.restart()
    step(NT, False, True, True)
    step(NT + 1, False, False, True)


def merge(nc, K):
    HALF = 512
    NL = NG + NE
    TAPS = [0, 8, 16, 24, CW]
    with ExitStack() as ctx:
        sb, ps = bufs(nc, ctx, "d_")
        wa, wc, wo = sb("w_attn", [P, KF, D]), sb("w_conv", [P, KF, D]), sb("w_o", [P, KD, D])
        wr = sb("w_router", [P, KD, NL])
        br = sb("b_router", [P, NL])
        mb, gain = sb("merge_bias", [P, 2, D]), sb("gain_ffn", [P, D])
        lng, lnb = sb("ln_gain", [P, CONV]), sb("ln_bias", [P, CONV])
        cwT, cbT = sb("conv_tapsT", [P, NCH, CW]), sb("conv_biasT", [P, NCH])
        hT, oT, zin = sb("hT", [P, KD, P]), sb("oT", [P, KF, P]), sb("conv_in", [P, NCH, HALO + P])
        acc = sb("conv_acc", [P, NCH, P])
        st, mv = sb("bn_stats", [P, 6]), sb("bn_mv", [P, 2])
        va, rs, eps = sb("var_eps", [P, 1]), sb("rstd_ln", [P, 1]), sb("eps", [P, 1])
        ln, lg, crow = sb("ln", [P, CONV]), sb("ln_sig", [P, CONV]), sb("c_rows", [P, CONV])
        cT = sb("cT", [P, NCH, P])
        gt = sb("gates_half", [P, 2, HALF])
        pa, pc = sb("part_a", [P, HALF]), sb("part_c", [P, HALF])
        m, mT = sb("mixed", [P, D]), sb("mixedT", [P, KD, P])
        xt, x2, junk = sb("x_rows", [P, D]), sb("x2_rows", [P, D]), sb("squares", [P, D])
        h2, h2T = sb("h2_rows", [P, D]), sb("h2T", [P, KD, P])
        ssq, ms, rstd = sb("ssq", [P, 1]), sb("ms", [P, 1]), sb("rstd", [P, 1])
        G = [ps(f"G{i}", [P, HALF]) for i in range(2)]
        Y = [ps(f"Y{i}", [P, HALF]) for i in range(2)]
        X = [ps(f"X{i}", [P, HALF]) for i in range(2)]
        T = [ps(f"T{i}", [P, 4, P]) for i in range(2)]
        S = Sems(nc, ctx, "d")
        s_c, s_cl, s_ct, s_cte = S("consts"), S("taps_loaded"), S("taps_psum"), S("taps")
        s_wa, s_wc, s_wo = S("w_attn"), S("w_conv"), S("w_o")
        s_hl, s_ol, s_zl, s_xl = S("hT_loaded"), S("oT_loaded"), S("conv_in_loaded"), S("x_loaded")
        s_cv, s_cb, s_var, s_rs, s_lx = S("convolved"), S("conv_psum"), S("var"), S("rstd_ln"), S("ln")
        s_lb, s_sg, s_cr, s_tc, s_cT = S("ln_psum_read"), S("ln_sig"), S("c_rows"), S("cT_psum"), S("cT")
        s_g, s_ga, s_gs, s_y, s_yu = S("gates_psum"), S("gates_biased"), S("gates"), S("y_psum"), S("y_used")
        s_m, s_tm, s_mT, s_x, s_x2 = S("mixed"), S("mT_psum"), S("mT"), S("x_psum"), S("x2")
        s_ssq, s_rstd, s_h2, s_th, s_hT = S("ssq"), S("rstd"), S("h2"), S("h2T_psum"), S("h2T")
        s_r, s_re, s_st, s_st2 = S("logits_psum"), S("logits"), S("x2_stored"), S("h2_stored")
        c_dve, c_pool, c_x = S("dve_chain"), S("pool_chain"), [S("none0"), S("none1"), S("none2")]
        block = ctx.enter_context(nc.Block())
        zT_view = K.zT_d.rearrange("(c p) t -> p c t", p=P)
        x_view = K.x[0].rearrange("(i p) d -> i p d", p=P)
        x2_view = K.x2_d.rearrange("(i p) d -> i p d", p=P)
        h2_view = K.h2_d.rearrange("(i p) d -> i p d", p=P)

        @block.sync
        def _(sp):
            sp.dma_start(zin[:, :, :], zT_view[:, :, 0:HALO + P]).then_inc(s_zl, 16)
            sp.dma_start(hT[:, :, :].rearrange("p k t -> p (k t)"),
                         K.hT_d[0].rearrange("p k t -> p (k t)")).then_inc(s_hl, 16)
            sp.dma_start(oT[:, :, :].rearrange("p k t -> p (k t)"),
                         K.oT_d[0].rearrange("p k t -> p (k t)")).then_inc(s_ol, 16)
            for t, v in ((mb[:, 0, :], K.merge_b[0, 0:D]), (mb[:, 1, :], K.merge_b[0, D:2 * D]),
                         (gain[:, :], K.ffn_norm_g[0]), (lng[:, :], K.conv_norm_g[0]),
                         (lnb[:, :], K.conv_norm_b[0]), (br[:, 0:NG], K.b_router_group[0]),
                         (br[:, NG:NL], K.b_router_expert[0])):
                sp.dma_start(t, v.partition_broadcast(P)).then_inc(s_c, 16)

            def step(j, now, lag1, lag2):
                if not now:
                    return
                if isinstance(j, int) and j == 0:
                    load_merge_weights(sp, K, 1)
                else:
                    sp.wait_ge(s_g, 4 * j)
                    sp.dma_start(hT[:, :, :].rearrange("p k t -> p (k t)"),
                                 K.hT_d[j].rearrange("p k t -> p (k t)")).then_inc(s_hl, 16)
                    sp.wait_ge(s_y, 2 * j)
                    sp.dma_start(oT[:, :, :].rearrange("p k t -> p (k t)"),
                                 K.oT_d[j].rearrange("p k t -> p (k t)")).then_inc(s_ol, 16)
                sp.wait_ge(s_cv, j + 1)
                sp.dma_start(zin[:, :, :], zT_view[:, :, ds((j + 1) * P, HALO + P)]).then_inc(s_zl, 16)
            lagged(sp, Chain(sp, c_x[0]), step)

        @block.scalar
        def _(act):
            act.dma_start(xt[:, :], x_view[0]).then_inc(s_xl, 16)
            act.dma_start(h2[0:CW, 0:CONV], K.conv_w[0]).then_inc(s_cl, 16)
            act.dma_start(h2[0:NCH, CONV:CONV + P], K.conv_b[0].rearrange("(c p) -> c p", p=P)).then_inc(s_cl, 16)
            act.dma_start(wa[:, :, :], K.w_attn_out[0].rearrange("(k p) n -> p k n", p=P)).then_inc(s_wa, 16)
            act.dma_start(wc[:, :, :], K.w_conv_out[0].rearrange("(k p) n -> p k n", p=P)).then_inc(s_wc, 16)
            act.dma_start(wo[:, :, :], K.w_out[0].rearrange("(k p) n -> p k n", p=P)).then_inc(s_wo, 16)
            act.dma_start(wr[:, :, 0:NG], K.w_router_group[0].rearrange("(k p) n -> p k n", p=P)).then_inc(s_wo, 16)
            act.dma_start(wr[:, :, NG:NL], K.w_router_expert[0].rearrange("(k p) n -> p k n", p=P))\
                .then_inc(s_wo, 16)
            act.wait_ge(s_ct, 1)
            nc.scalar.copy(cwT[:, :, :], T[0][:, :, 0:CW])
            nc.scalar.copy(cbT[:, :], T[0][:, 0, 64:64 + NCH]).then_inc(s_cte, 1)

            def sigmoids(j, half):
                act.wait_ge(s_ga, 4 * j + 2 * half + 2)
                nc.scalar.activation(gt[:, :, :], gt[:, :, :], ACT.Sigmoid).then_inc(s_gs, 1)

            def step(j, now, lag1, lag2):
                if now:
                    act.wait_ge(s_lx, j + 1)
                    nc.scalar.activation(lg[:, :], ln[:, :], ACT.Sigmoid).then_inc(s_sg, 1)
                    sigmoids(j, 0)
                    act.wait_ge(s_tc, j + 1)
                    nc.scalar.copy(cT[:, :, :], T[0][:, :, :]).then_inc(s_cT, 1)
                if lag1:
                    for n in range(2):
                        act.wait_ge(s_tm, 2 * (j - 1) + n + 1)
                        nc.scalar.copy(mT[:, 4 * n:4 * n + 4, :], T[n][:, :, :]).then_inc(s_mT, 1)
                if now:
                    sigmoids(j, 1)
                if lag2:
                    for n in range(2):
                        act.wait_ge(s_th, 2 * (j - 2) + n + 1)
                        nc.scalar.copy(h2T[:, 4 * n:4 * n + 4, :], T[n][:, :, :]).then_inc(s_hT, 1)
                if lag1:
                    act.wait_ge(s_x2, 2 * j)
                    nc.scalar.activation(junk[:, :], x2[:, :], ACT.Square, accum_out=ssq[:, :]).then_inc(s_ssq, 1)
                    act.dma_start(x2_view[j - 1], x2[:, :]).then_inc(s_st, 16)
                    if now:
                        act.dma_start(xt[:, :], x_view[j]).then_inc(s_xl, 16)
                    act.wait_ge(s_h2, j)
                    act.dma_start(h2_view[j - 1], h2[:, :]).then_inc(s_st2, 16)
            lagged(act, Chain(act, c_x[1]), step)
            act.wait_ge(s_st, 16 * NT)
            act.wait_ge(s_st2, 16 * NT)

        @block.gpsimd
        def _(pool):
            c = Chain(pool, c_pool)
            c.mark(nc.gpsimd.memset(eps[:, :], EPS))
            c.sync()

            def step(j, now, lag1, lag2):
                if now:
                    pool.wait_ge(s_var, j + 1)
                    c.mark(nc.gpsimd.tensor_tensor(va[:, :], mv[:, 1:2], eps[:, :], ALU.add))
                    c.sync()
                    nc.gpsimd.tensor_tensor(rs[:, :], va[:, :], K.mhalf[:, 0:1], ALU.pow).then_inc(s_rs, 1)
                if lag1:
                    pool.wait_ge(s_ssq, j)
                    c.mark(nc.gpsimd.tensor_tensor(ms[:, :], ssq[:, :], K.inv_d[:, 0:1], ALU.mult))
                    c.sync()
                    c.mark(nc.gpsimd.tensor_tensor(ms[:, :], ms[:, :], eps[:, :], ALU.add))
                    c.sync()
                    nc.gpsimd.tensor_tensor(rstd[:, :], ms[:, :], K.mhalf[:, 0:1], ALU.pow).then_inc(s_rstd, 1)
            lagged(pool, c, step)

        @block.tensor
        def _(pe):
            pe.wait_ge(s_cl, 32)
            for k in range(NCH):
                nc.tensor.transpose(T[0][:, k, 0:CW], h2[0:CW, ts(k, P)], K.ident[0:CW, 0:CW])
            nc.tensor.transpose(T[0][:, 0, 64:64 + NCH], h2[0:NCH, CONV:CONV + P], K.ident[0:NCH, 0:NCH])\
                .then_inc(s_ct, 1)
            pe.wait_ge(s_cte, 1)

            def gates(j, half):
                wait_if(pe, s_ga, 4 * j + 2 * half)
                for b in range(2):
                    for k in range(KD):
                        last = nc.tensor.matmul(G[b][:, :], hT[:, k, :], K.wm[half][:, k, ts(b, HALF)],
                                                start=(k == 0), stop=(k == KD - 1))
                    last.then_inc(s_g, 1)

            def outputs(j, half):
                wait_if(pe, s_yu, 4 * j + 2 * half)
                for b, (lhs, w) in enumerate(((oT, wa), (cT, wc))):
                    for k in range(KF):
                        last = nc.tensor.matmul(Y[b][:, :], lhs[:, k, :], w[:, k, ts(half, HALF)],
                                                start=(k == 0), stop=(k == KF - 1))
                last.then_inc(s_y, 1)

            def step(j, now, lag1, lag2):
                static = isinstance(j, int)
                if static and j == 0:
                    pe.wait_ge(K.s_wm, 32)
                    pe.wait_ge(s_hl, 16)
                    gates(0, 0)
                if now:
                    pe.wait_ge(s_cv, j + 1)
                    wait_if(pe, s_lb, j)
                    for k in range(NCH):
                        last = nc.tensor.transpose(T[1][:, k, :], acc[:, k, :], K.ident[:, :])
                    last.then_inc(s_cb, 1)
                    if not (static and j == 0):
                        pe.wait_ge(s_hl, 16 * j + 16)
                        gates(j, 0)
                    pe.wait_ge(s_cr, j + 1)
                    if lag2:
                        pe.wait_ge(s_re, j - 1)
                    for k in range(NCH):
                        last = nc.tensor.transpose(T[0][:, k, :], crow[:, ts(k, P)], K.ident[:, :])
                    last.then_inc(s_tc, 1)
                    if static and j == 0:
                        pe.wait_ge(s_wa, 16)
                        pe.wait_ge(s_wc, 16)
                    pe.wait_ge(s_ol, 16 * j + 16)
                    pe.wait_ge(s_cT, j + 1)
                    outputs(j, 0)
                if lag1:
                    pe.wait_ge(s_m, j)
                    if now:
                        pe.wait_ge(s_lb, j + 1)
                    else:
                        pe.wait_ge(s_re, j - 1)
                    for n in range(2):
                        for k in range(4):
                            last = nc.tensor.transpose(T[n][:, k, :], m[:, ts(4 * n + k, P)], K.ident[:, :])
                        last.then_inc(s_tm, 1)
                if now:
                    if static and j == 0:
                        pe.wait_ge(K.s_wm, 64)
                    gates(j, 1)
                    outputs(j, 1)
                if lag1:
                    pe.wait_ge(s_mT, 2 * j)
                if lag2:
                    pe.wait_ge(s_h2, j - 1)
                    for n in range(2):
                        for k in range(4):
                            last = nc.tensor.transpose(T[n][:, k, :], h2[:, ts(4 * n + k, P)], K.ident[:, :])
                        last.then_inc(s_th, 1)
                if lag1:
                    if static and j == 1:
                        pe.wait_ge(s_wo, 48)
                    wait_if(pe, s_x2, 2 * (j - 1))
                    for b in range(2):
                        for k in range(KD):
                            last = nc.tensor.matmul(X[b][:, :], mT[:, k, :], wo[:, k, ts(b, HALF)],
                                                    start=(k == 0), stop=(k == KD - 1))
                        last.then_inc(s_x, 1)
                if lag2:
                    pe.wait_ge(s_hT, 2 * (j - 1))
                    for k in range(KD):
                        last = nc.tensor.matmul(T[0][:, 0, 0:NL], h2T[:, k, :], wr[:, k, :],
                                                start=(k == 0), stop=(k == KD - 1))
                    last.then_inc(s_r, 1)
            lagged(pe, Chain(pe, c_x[2]), step)

        @block.vector
        def _(dve):
            c = Chain(dve, c_dve)

            def put(ins):
                c.mark(ins)
                c.sync()

            def convolve(part):
                for t in range(TAPS[part], TAPS[part + 1]):
                    for k in range(NCH):
                        c.sync(NCH - 1)
                        src = zin[:, k, t:t + P]
                        if t == 0:
                            ins = nc.vector.tensor_scalar(acc[:, k, :], src, cwT[:, k, 0:1], cbT[:, k:k + 1],
                                                          ALU.mult, ALU.add)
                        else:
                            ins = nc.vector.scalar_tensor_tensor(acc[:, k, :], src, cwT[:, k, t:t + 1],
                                                                 acc[:, k, :], ALU.mult, ALU.add)
                        if t == CW - 1 and k == NCH - 1:
                            ins.then_inc(s_cv, 1)
                        else:
                            c.mark(ins)

            def bias(j, half):
                for b in range(2):
                    dve.wait_ge(s_g, 4 * j + 2 * half + b + 1)
                    nc.vector.tensor_tensor(gt[:, b, :], G[b][:, :], mb[:, b, ts(half, HALF)],
                                            ALU.add).then_inc(s_ga, 1)

            def mix(j, half):
                dve.wait_ge(s_gs, 2 * j + half + 1)
                dve.wait_ge(s_y, 2 * j + half + 1)
                nc.vector.tensor_tensor(pa[:, :], gt[:, 0, :], Y[0][:, :], ALU.mult).then_inc(s_yu, 1)
                nc.vector.tensor_tensor(pc[:, :], gt[:, 1, :], Y[1][:, :], ALU.mult).then_inc(s_yu, 1)
                if half == 0:
                    wait_if(dve, s_tm, 2 * j)
                dve.wait_ge(s_yu, 4 * j + 2 * half + 2)
                ins = nc.vector.tensor_tensor(m[:, ts(half, HALF)], pa[:, :], pc[:, :], ALU.add)
                if half:
                    ins.then_inc(s_m, 1)

            def step(j, now, lag1, lag2):
                if now:
                    dve.wait_ge(s_cb, j + 1)
                    put(nc.vector.bn_stats(st[:, :], T[1][:, :, :].rearrange("p c n -> p (c n)")))
                    nc.vector.bn_aggr(mv[:, :], st[:, :]).then_inc(s_var, 1)
                    dve.wait_ge(s_zl, 16 * j + 32)
                    convolve(0)
                    dve.wait_ge(s_rs, j + 1)
                    nc.vector.tensor_scalar(ln[:, :], T[1][:, :, :].rearrange("p c n -> p (c n)"), mv[:, 0:1],
                                            rs[:, 0:1], ALU.subtract, ALU.mult).then_inc(s_lb, 1)
                    dve.wait_ge(s_lb, j + 1)
                    put(nc.vector.tensor_tensor(ln[:, :], ln[:, :], lng[:, :], ALU.mult))
                    nc.vector.tensor_tensor(ln[:, :], ln[:, :], lnb[:, :], ALU.add).then_inc(s_lx, 1)
                    bias(j, 0)
                    dve.wait_ge(s_sg, j + 1)
                    wait_if(dve, s_tc, j)
                    nc.vector.tensor_tensor(crow[:, :], ln[:, :], lg[:, :], ALU.mult).then_inc(s_cr, 1)
                    convolve(1)
                    mix(j, 0)
                    convolve(2)
                    bias(j, 1)
                    mix(j, 1)
                    convolve(3)
                if lag1:
                    dve.wait_ge(s_xl, 16 * j)
                    wait_if(dve, s_st, 16 * (j - 1))
                    for b in range(2):
                        dve.wait_ge(s_x, 2 * (j - 1) + b + 1)
                        nc.vector.tensor_tensor(x2[:, ts(b, HALF)], X[b][:, :], xt[:, ts(b, HALF)],
                                                ALU.add).then_inc(s_x2, 1)
                if lag2:
                    dve.wait_ge(s_r, j - 1)
                    nc.vector.tensor_tensor(K.lg[:, ds(j - 2, 1), :].rearrange("p a n -> p (a n)"),
                                            T[0][:, 0, 0:NL], br[:, :], ALU.add).then_inc(s_re, 1)
                if lag1:
                    dve.wait_ge(s_rstd, j)
                    wait_if(dve, s_st2, 16 * (j - 1))
                    wait_if(dve, s_th, 2 * (j - 1))
                    nc.vector.scalar_tensor_tensor(h2[:, :], x2[:, :], rstd[:, 0:1], gain[:, :],
                                                   ALU.mult, ALU.mult).then_inc(s_h2, 1)
            dve.sem_inc(s_re, 1)
            dve.wait_ge(s_c, 16 * 7)
            dve.wait_ge(s_cte, 1)
            dve.wait_ge(s_zl, 16)
            for part in range(4):
                convolve(part)
            lagged(dve, c, step)


def load_expert(eng, K, e, par):
    for buf, w, sem in ((K.wg[par], K.w_exp_gate, K.s_gu[par]), (K.wu[par], K.w_exp_up, K.s_gu[par]),
                        (K.wd[par], K.w_exp_down, K.s_wd[par])):
        eng.dma_start(buf[:, :, :], w[0].rearrange("e (k p) n -> e p k n", p=P)[e]).then_inc(sem, 16)


def route(nc, K):
    with ExitStack() as ctx:
        sb, ps = bufs(nc, ctx, "r_")
        NL = NG + NE
        desc, thr = sb("descending", [P, EPG]), sb("block_thresholds", [P, NT - 1])
        io64, io128 = sb("iota_blocks", [P, MAX_BLK]), sb("iota_slots", [P, P])
        tri, ones = sb("before", [P, P], BF16), sb("ones", [P, P], BF16)
        gm, gd, gs, pg = sb("gmax", [P, NT]), sb("gdiff", [P, NT, NG]), sb("gsum", [P, NT]), sb("pg", [P, NT])
        og, v4 = sb("onehot_g", [P, NT, NG]), sb("v4", [P, NT, NG])
        le, sel, v8 = sb("le", [P, NT, EPG]), sb("le_all", [P, NT, EPG, NG]), sb("v8", [P, NT, EPG])
        o1, o2 = sb("onehot_1", [P, NT, EPG]), sb("onehot_2", [P, NT, EPG])
        m1, m2, mx = sb("m1", [P, NT]), sb("m2", [P, NT]), sb("mx", [P, NT])
        e2, den = sb("e2", [P, NT]), sb("den", [P, NT])
        E = [sb(f"E{k}", [P, NT, NE]) for k in range(2)]
        Eb = sb("E_both", [P, NT, NE], BF16)
        cum = sb("tiles_before", [P, NT + 1, NE])
        nb, nbc, bs = sb("nblocks", [P, NE]), sb("over", [P, NE, NT - 1]), sb("block_start", [P, NE + 1])
        base, rank = sb("base", [P, NE]), sb("rank", [P, NT, NE])
        prod = sb("prod", [P, NT, NE])
        slot, blk, off = sb("slot", [P, 2, NT]), sb("blk", [P, 2, NT]), sb("off", [P, 2, NT])
        A = [sb(f"A{k}", [P, NT, P]) for k in range(2)]
        B = [sb(f"B{k}", [P, NT, MAX_BLK]) for k in range(2)]
        R, TT, IX = ps("R", [P, NT, NE]), ps("TT", [P, NT, NE]), ps("IX", [P, 512])
        S = Sems(nc, ctx, "r")
        s_k, s_p, s_d, s_gd, s_ex, s_m, s_ex2 = (S("consts"), S("pool"), S("dve"), S("gdiff"), S("gexp"), S("mdiff"),
                                                 S("mexp"))
        s_e, s_r, s_ab, s_ix = S("onehots"), S("ranks_psum"), S("slots"), S("idx_psum")
        block = ctx.enter_context(nc.Block())

        @block.gpsimd
        def _(pool):
            c = Chain(pool, s_p)

            def put(ins):
                c.mark(ins)
                c.sync()
            io = dict(channel_multiplier=0, allow_small_or_imprecise_dtypes=True)
            c.mark(nc.gpsimd.iota(desc[:, :], [[-1, EPG]], base=EPG, **io))
            c.mark(nc.gpsimd.iota(thr[:, :], [[P, NT - 1]], base=P, **io))
            c.mark(nc.gpsimd.iota(io64[:, :], [[1, MAX_BLK]], base=0, **io))
            c.mark(nc.gpsimd.iota(io128[:, :], [[1, P]], base=0, **io))
            c.mark(nc.gpsimd.memset(ones[:, :], 1.0))
            put(nc.gpsimd.memset(tri[:, :], 1.0))
            put(nc.gpsimd.affine_select(out=tri[:, :], in_=tri[:, :], compare_op=ALU.is_gt, fill=0.0,
                                        base=0, pattern=[[1, P]], channel_multiplier=-1))
            nc.gpsimd.memset(K.idx[:, MAX_BLK:MAX_BLK + 1], 0).then_inc(s_k, 1)

        @block.sync
        def _(sp):
            for e in range(2):
                load_expert(sp, K, e, e)

        @block.scalar
        def _(act):
            act.wait_ge(s_gd, 1)
            nc.scalar.activation(gd[:, :, :], gd[:, :, :], ACT.Exp).then_inc(s_ex, 1)
            act.wait_ge(s_m, 1)
            nc.scalar.activation(e2[:, :], e2[:, :], ACT.Exp).then_inc(s_ex2, 1)

        @block.tensor
        def _(pe):
            pe.wait_ge(s_k, 1)
            pe.wait_ge(s_e, 1)
            eb = Eb[:, :, :].rearrange("p t e -> p (t e)")
            nc.tensor.matmul(R[:, :, :].rearrange("p t e -> p (t e)"), tri[:, :], eb, start=True, stop=True)
            nc.tensor.matmul(TT[:, :, :].rearrange("p t e -> p (t e)"), ones[:, :], eb,
                             start=True, stop=True).then_inc(s_r, 1)
            pe.wait_ge(s_ab, 1)
            for k in range(2):
                for t in range(NT):
                    last = nc.tensor.matmul(IX[:, 0:MAX_BLK], A[k][:, t, :], B[k][:, t, :],
                                            start=(k == 0 and t == 0), stop=(k == 1 and t == NT - 1))
            last.then_inc(s_ix, 1)

        @block.vector
        def _(dve):
            V = nc.vector
            c = Chain(dve, s_d)

            def put(ins):
                c.mark(ins)
                c.sync()

            def up(t, n):
                return t.unsqueeze(2).to_broadcast([P, NT, n])

            def first_max(dst, src, m, tmp, n):
                put(V.tensor_reduce(m[:, :], src, AX, ALU.max))
                put(V.tensor_tensor(tmp[:, :, :], src, up(m[:, :], n), ALU.is_equal))
                put(V.tensor_tensor(tmp[:, :, :], tmp[:, :, :],
                                    desc[:, 0:n].unsqueeze(1).to_broadcast([P, NT, n]), ALU.mult))
                put(V.tensor_reduce(mx[:, :], tmp[:, :, :], AX, ALU.max))
                put(V.tensor_tensor(dst[:, :, :], tmp[:, :, :], up(mx[:, :], n), ALU.is_equal))
            dve.wait_ge(s_k, 1)
            lgg = K.lg[:, :, 0:NG]
            first_max(og, lgg, gm, v4, NG)
            V.tensor_tensor(gd[:, :, :], lgg, up(gm[:, :], NG), ALU.subtract).then_inc(s_gd, 1)
            lge = K.lg[:, :, NG:NL].rearrange("p t (g e) -> p t e g", g=NG)
            for t in range(NT):
                c.mark(V.tensor_tensor(sel[:, t, :, :], lge[:, t, :, :],
                                       og[:, t:t + 1, :].to_broadcast([P, EPG, NG]), ALU.mult))
            c.sync()
            put(V.tensor_reduce(le[:, :, :], sel[:, :, :, :], AX, ALU.add))
            first_max(o1, le[:, :, :], m1, v8, EPG)
            put(V.scalar_tensor_tensor(le[:, :, :], o1[:, :, :], NEG, le[:, :, :], ALU.mult, ALU.add))
            first_max(o2, le[:, :, :], m2, v8, EPG)
            V.tensor_tensor(e2[:, :], m2[:, :], m1[:, :], ALU.subtract).then_inc(s_m, 1)
            for k, o in enumerate((o1, o2)):
                for g in range(NG):
                    c.mark(V.tensor_tensor(E[k][:, :, g * EPG:(g + 1) * EPG], o[:, :, :],
                                           og[:, :, g:g + 1].to_broadcast([P, NT, EPG]), ALU.mult))
            c.sync()
            V.tensor_tensor(Eb[:, :, :], E[0][:, :, :], E[1][:, :, :], ALU.add).then_inc(s_e, 1)
            dve.wait_ge(s_ex, 1)
            put(V.tensor_reduce(gs[:, :], gd[:, :, :], AX, ALU.add))
            put(V.reciprocal(pg[:, :], gs[:, :]))
            dve.wait_ge(s_ex2, 1)
            put(V.tensor_scalar(den[:, :], e2[:, :], 1.0, None, ALU.add))
            put(V.reciprocal(gs[:, :], den[:, :]))
            put(V.tensor_tensor(K.wts[:, 0, :], pg[:, :], gs[:, :], ALU.mult))
            c.mark(V.tensor_tensor(K.wts[:, 1, :], K.wts[:, 0, :], e2[:, :], ALU.mult))
            put(V.memset(cum[:, 0, :], 0.0))
            dve.wait_ge(s_r, 1)
            for t in range(NT):
                put(V.tensor_tensor(cum[:, t + 1, :], cum[:, t, :], TT[:, t, :], ALU.add))
            put(V.tensor_tensor(nbc[:, :, :], cum[:, NT, :].unsqueeze(2).to_broadcast([P, NE, NT - 1]),
                                thr[:, :].unsqueeze(1).to_broadcast([P, NE, NT - 1]), ALU.is_gt))
            put(V.tensor_reduce(nb[:, :], nbc[:, :, :], AX, ALU.add))
            put(V.tensor_scalar(nb[:, :], nb[:, :], 1.0, None, ALU.add))
            put(V.memset(bs[:, 0:1], 0.0))
            for e in range(NE):
                put(V.tensor_tensor(bs[:, e + 1:e + 2], bs[:, e:e + 1], nb[:, e:e + 1], ALU.add))
            c.mark(V.tensor_copy(K.starts[:, :], bs[0:1, :]))
            put(V.tensor_scalar(base[:, :], bs[:, 0:NE], float(P), None, ALU.mult))
            put(V.tensor_tensor(rank[:, :, :], R[:, :, :], cum[:, 0:NT, :], ALU.add))
            put(V.tensor_tensor(rank[:, :, :], rank[:, :, :],
                                base[:, :].unsqueeze(1).to_broadcast([P, NT, NE]), ALU.add))
            for k in range(2):
                put(V.tensor_tensor(prod[:, :, :], E[k][:, :, :], rank[:, :, :], ALU.mult))
                put(V.tensor_reduce(slot[:, k, :], prod[:, :, :], AX, ALU.add))
                put(V.tensor_scalar(off[:, k, :], slot[:, k, :], 1.0 / P, None, ALU.mult))
                put(V.tensor_tensor(B[k][:, :, :], io64[:, :].unsqueeze(1).to_broadcast([P, NT, MAX_BLK]),
                                    up(off[:, k, :], MAX_BLK), ALU.is_le))
                put(V.tensor_reduce(blk[:, k, :], B[k][:, :, :], AX, ALU.add))
                put(V.tensor_scalar(blk[:, k, :], blk[:, k, :], -1.0, None, ALU.add))
                put(V.scalar_tensor_tensor(off[:, k, :], blk[:, k, :], -float(P), slot[:, k, :], ALU.mult, ALU.add))
                put(V.tensor_tensor(B[k][:, :, :], io64[:, :].unsqueeze(1).to_broadcast([P, NT, MAX_BLK]),
                                    up(blk[:, k, :], MAX_BLK), ALU.is_equal))
                put(V.tensor_tensor(B[k][:, :, :], B[k][:, :, :], up(K.tpos[:, :], MAX_BLK), ALU.mult))
                put(V.tensor_tensor(A[k][:, :, :], io128[:, :].unsqueeze(1).to_broadcast([P, NT, P]),
                                    up(off[:, k, :], P), ALU.is_equal))
            put(V.tensor_copy(K.slots[:, :, :], slot[:, :, :]))
            V.memset(gm[:, :], 0.0).then_inc(s_ab, 1)
            dve.wait_ge(s_ix, 1)
            V.tensor_copy(K.idx[:, 0:MAX_BLK], IX[:, 0:MAX_BLK])


def experts(nc, K):
    with ExitStack() as ctx:
        sb, ps = bufs(nc, ctx, "e_")
        wg, wu, wd = K.wg, K.wu, K.wd
        xg, xT = sb("x_gathered", [P, D]), sb("xT", [P, KD, P])
        cur = sb("idx_now", [P, 1], U32)
        sg, h, hT, y = sb("silu", [P, FF]), sb("h_rows", [P, FF]), sb("hT", [P, KF, P]), sb("y_rows", [P, D])
        G, U = ps("G", [P, FF]), ps("U", [P, FF])
        T = [ps(f"T{i}", [P, 4, P]) for i in range(2)]
        TH = ps("TH", [P, KF, P])
        Y = [ps(f"Y{i}", [P, 512]) for i in range(2)]
        S = Sems(nc, ctx, "e")
        s_gu, s_wd = K.s_gu, K.s_wd
        s_ix, s_xg, s_tx, s_xT = S("idx"), S("gathered"), S("xT_psum"), S("xT")
        s_g, s_u, s_sg, s_h = S("gate_psum"), S("up_psum"), S("silu"), S("h")
        s_th, s_hT, s_dn, s_ye, s_ys = S("hT_psum"), S("hT"), S("down_psum"), S("y_rows"), S("y_stored")
        c_x = [S(f"none{i}") for i in range(5)]
        block = ctx.enter_context(nc.Block())
        y_view = K.y_d.rearrange("(b p) n -> b p n", p=P)

        def nblocks(eng):
            return eng.value_load(K.starts[0:1, NE:NE + 1], min_val=NE, max_val=MAX_BLK)

        @block.sync
        def _(sp):
            with sp.Fori(1, NE // 2) as ep:
                for par in range(2):
                    e = ep * 2 + par
                    done = sp.value_load(K.starts[0:1, ds(e - 1, 1)], min_val=1, max_val=MAX_BLK)
                    sp.wait_ge(s_dn, done * 2)
                    load_expert(sp, K, e, par)
            sp.dma_start(K.wpp[:, :, :], K.w_ple_proj[0].rearrange("(k p) n -> p k n", p=P)).then_inc(K.s_wpl, 16)
            sp.dma_start(K.wpg[:, :, :], K.w_ple_gate[0].rearrange("(k p) n -> p k n", p=P)).then_inc(K.s_wpl, 16)

        @block.gpsimd
        def _(pool):
            c = Chain(pool, s_ix)

            def gather(g):
                c.mark(nc.gpsimd.tensor_copy(cur[:, :], K.idx[:, ds(g, 1)]))
                c.sync()
                pool.indirect_dma_start(xg[:, :], None, K.h2_d, bass.IndirectOffsetOnAxis(cur[:, 0:1], 0))\
                    .then_inc(s_xg, 16)
            gather(0)
            c.restart()
            n = nblocks(pool)
            with pool.Fori(0, n) as g:
                pool.wait_ge(s_tx, g * 2 + 2)
                gather(g + 1)
                c.restart()
            pool.wait_ge(s_xg, n * 16 + 16)

        @block.tensor
        def _(pe):
            def transpose_x():
                for n in range(2):
                    for k in range(4):
                        last = nc.tensor.transpose(T[n][:, k, :], xg[:, ts(4 * n + k, P)], K.ident[:, :])
                    last.then_inc(s_tx, 1)
            pe.wait_ge(s_xg, 16)
            transpose_x()
            with pe.Fori(0, NE // 2) as ep:
                for par in range(2):
                    e = ep * 2 + par
                    b0 = pe.value_load(K.starts[0:1, ds(e, 1)], min_val=0, max_val=MAX_BLK - 1)
                    b1 = pe.value_load(K.starts[0:1, ds(e + 1, 1)], min_val=1, max_val=MAX_BLK)
                    with pe.Fori(b0, b1) as g:
                        pe.wait_ge(s_gu[par], ep * 32 + 32)
                        pe.wait_ge(s_xT, g * 2 + 2)
                        pe.wait_ge(s_h, g + 1)
                        for k in range(KD):
                            last = nc.tensor.matmul(G[:, :], xT[:, k, :], wg[par][:, k, :],
                                                    start=(k == 0), stop=(k == KD - 1))
                        last.then_inc(s_g, 1)
                        for k in range(KD):
                            last = nc.tensor.matmul(U[:, :], xT[:, k, :], wu[par][:, k, :],
                                                    start=(k == 0), stop=(k == KD - 1))
                        last.then_inc(s_u, 1)
                        pe.wait_ge(s_xg, g * 16 + 32)
                        transpose_x()
                        pe.wait_ge(s_h, g + 2)
                        for k in range(KF):
                            last = nc.tensor.transpose(TH[:, k, :], h[:, ts(k, P)], K.ident[:, :])
                        last.then_inc(s_th, 1)
                        pe.wait_ge(s_wd[par], ep * 16 + 16)
                        pe.wait_ge(s_hT, g + 1)
                        pe.wait_ge(s_ye, g * 2 + 2)
                        for b in range(2):
                            for k in range(KF):
                                last = nc.tensor.matmul(Y[b][:, :], hT[:, k, :], wd[par][:, k, ts(b, 512)],
                                                        start=(k == 0), stop=(k == KF - 1))
                            last.then_inc(s_dn, 1)

        @block.scalar
        def _(act):
            n = nblocks(act)
            act.sem_inc(s_ye, 2)
            act.sem_inc(s_ys, 16)
            act.wait_ge(s_tx, 1)
            nc.scalar.copy(xT[:, 0:4, :], T[0][:, :, :]).then_inc(s_xT, 1)
            with act.Fori(0, n) as g:
                act.wait_ge(s_g, g + 1)
                nc.scalar.activation(sg[:, :], G[:, :], ACT.Silu).then_inc(s_sg, 1)
                act.wait_ge(s_tx, g * 2 + 3)
                nc.scalar.copy(xT[:, 0:4, :], T[0][:, :, :]).then_inc(s_xT, 1)
                act.wait_ge(s_th, g + 1)
                nc.scalar.copy(hT[:, :, :], TH[:, :, :]).then_inc(s_hT, 1)
                act.wait_ge(s_ys, g * 16 + 16)
                act.wait_ge(s_dn, g * 2 + 1)
                nc.scalar.copy(y[:, 0:512], Y[0][:, :]).then_inc(s_ye, 1)
                act.wait_ge(s_ye, g * 2 + 4)
                act.dma_start(y_view[g], y[:, :]).then_inc(s_ys, 16)
            act.wait_ge(s_ys, n * 16 + 16)
            nc.scalar.copy(sg[:, 0:1], y[:, 0:1])

        @block.vector
        def _(dve):
            n = nblocks(dve)
            dve.sem_inc(s_h, 1)
            dve.wait_ge(s_tx, 2)
            nc.vector.tensor_copy(xT[:, 4:8, :], T[1][:, :, :]).then_inc(s_xT, 1)
            with dve.Fori(0, n) as g:
                dve.wait_ge(s_sg, g + 1)
                dve.wait_ge(s_u, g + 1)
                nc.vector.tensor_tensor(h[:, :], U[:, :], sg[:, :], ALU.mult).then_inc(s_h, 1)
                dve.wait_ge(s_tx, g * 2 + 4)
                nc.vector.tensor_copy(xT[:, 4:8, :], T[1][:, :, :]).then_inc(s_xT, 1)
                dve.wait_ge(s_ys, g * 16 + 16)
                dve.wait_ge(s_dn, g * 2 + 2)
                nc.vector.tensor_copy(y[:, 512:D], Y[1][:, :]).then_inc(s_ye, 1)


def combine(nc, K):
    KP = PLE // P
    with ExitStack() as ctx:
        sb, ps = bufs(nc, ctx, "f_")
        wg, wp = K.wpg, K.wpp
        gain, bg = sb("gain", [P, D]), sb("b_gate", [P, D])
        cur = sb("idx_now", [P, 2], U32)
        y = [sb(f"y{k}", [P, D]) for k in range(2)]
        x2, p, x3, keep = sb("x2", [P, D]), sb("p_rows", [P, PLE]), sb("x3", [P, D]), sb("x3_keep", [P, D])
        junk, h3, hT, pT = sb("squares", [P, D]), sb("h3", [P, D]), sb("h3T", [P, KD, P]), sb("pT", [P, KP, P])
        gt, o = sb("gate", [P, D]), sb("out_rows", [P, D])
        eps, ssq, ms, rstd = sb("eps", [P, 1]), sb("ssq", [P, 1]), sb("ms", [P, 1]), sb("rstd", [P, 1])
        T = [ps(f"T{i}", [P, 4, P]) for i in range(2)]
        TP = ps("TP", [P, 4, P])
        G = [ps(f"G{i}", [P, 512]) for i in range(2)]
        Q = [ps(f"Q{i}", [P, 512]) for i in range(2)]
        S = Sems(nc, ctx, "f")
        s_c, s_ld, s_y, s_x3, s_ssq, s_rstd = (S("consts"), S("loaded"), S("y"),
                                                          S("x3"), S("ssq"), S("rstd"))
        s_h, s_t, s_hT, s_g, s_q, s_ga, s_gs = (S("h3"), S("T_psum"), S("hT"), S("gate_psum"), S("proj_psum"),
                                                S("gate_biased"), S("gate"))
        s_gm, s_o, s_st = S("gated"), S("out_rows"), S("out_stored")
        c_dve, c_pool, c_x = S("dve_chain"), S("pool_chain"), [S("none0"), S("none1"), S("none2")]
        s_kp = S("kept")
        block = ctx.enter_context(nc.Block())
        x2_view = K.x2_d.rearrange("(i p) d -> i p d", p=P)
        p_view = K.p[0, 0].rearrange("(i p) d -> i p d", p=P)
        out_view = K.out[0].rearrange("(i p) d -> i p d", p=P)

        def lag1(eng, chain, step):
            step(0, True, False)
            chain.restart()
            with eng.Fori(1, NT) as j:
                step(j, True, True)
                chain.restart()
            step(NT, False, True)

        @block.sync
        def _(sp):
            for t, v in ((gain[:, :], K.ple_norm_g[0]), (bg[:, :], K.b_ple_gate[0])):
                sp.dma_start(t, v.partition_broadcast(P)).then_inc(s_c, 16)

            def step(j, now, last):
                if now:
                    wait_if(sp, s_x3, j)
                    sp.dma_start(x2[:, :], x2_view[j]).then_inc(s_ld, 16)
                    wait_if(sp, s_t, 3 * j)
                    sp.dma_start(p[:, :], p_view[j]).then_inc(s_ld, 16)
                if last:
                    sp.wait_ge(s_o, j)
                    sp.dma_start(out_view[j - 1], o[:, :]).then_inc(s_st, 16)
            sp.sem_inc(s_st, 16)
            lag1(sp, Chain(sp, c_x[0]), step)
            sp.wait_ge(s_st, 16 * NT + 16)

        @block.gpsimd
        def _(pool):
            c = Chain(pool, c_pool)
            c.mark(nc.gpsimd.memset(eps[:, :], EPS))
            c.sync()

            def gathers(j):
                wait_if(pool, s_x3, j)
                for k in range(2):
                    c.mark(nc.gpsimd.tensor_copy(cur[:, k:k + 1], K.slots[:, k, ds(j, 1)]))
                c.sync()
                for k in range(2):
                    pool.indirect_dma_start(y[k][:, :], None, K.y_d, bass.IndirectOffsetOnAxis(cur[:, k:k + 1], 0))\
                        .then_inc(s_y, 16)

            def step(j, now, last):
                if now:
                    pool.wait_ge(s_ssq, j + 1)
                    c.mark(nc.gpsimd.tensor_tensor(ms[:, :], ssq[:, :], K.inv_d[:, 0:1], ALU.mult))
                    c.sync()
                    c.mark(nc.gpsimd.tensor_tensor(ms[:, :], ms[:, :], eps[:, :], ALU.add))
                    c.sync()
                    nc.gpsimd.tensor_tensor(rstd[:, :], ms[:, :], K.mhalf[:, 0:1], ALU.pow).then_inc(s_rstd, 1)
                    if not isinstance(j, int) or j < NT - 1:
                        gathers(j + 1)
            gathers(0)
            step(0, True, False)
            c.restart()
            with pool.Fori(1, NT - 1) as j:
                step(j, True, True)
                c.restart()
            step(NT - 1, True, True)
            pool.wait_ge(s_y, 32 * NT)

        @block.scalar
        def _(act):
            def step(j, now, last):
                if now:
                    act.wait_ge(s_x3, j + 1)
                    nc.scalar.activation(junk[:, :], x3[:, :], ACT.Square, accum_out=ssq[:, :]).then_inc(s_ssq, 1)
                    act.wait_ge(s_t, 3 * j + 1)
                    nc.scalar.copy(pT[:, :, :], TP[:, 0:KP, :]).then_inc(s_hT, 1)
                    for n in range(2):
                        act.wait_ge(s_t, 3 * j + n + 2)
                        nc.scalar.copy(hT[:, 4 * n:4 * n + 4, :], T[n][:, :, :]).then_inc(s_hT, 1)
                if last:
                    act.wait_ge(s_ga, 2 * j)
                    nc.scalar.activation(gt[:, :], gt[:, :], ACT.Sigmoid).then_inc(s_gs, 1)
            lag1(act, Chain(act, c_x[1]), step)

        @block.tensor
        def _(pe):
            def step(j, now, last):
                if not now:
                    return
                pe.wait_ge(s_ld, 32 * j + 32)
                for k in range(KP):
                    lastt = nc.tensor.transpose(TP[:, k, :], p[:, ts(k, P)], K.ident[:, :])
                lastt.then_inc(s_t, 1)
                pe.wait_ge(s_h, j + 1)
                for n in range(2):
                    for k in range(4):
                        lastt = nc.tensor.transpose(T[n][:, k, :], h3[:, ts(4 * n + k, P)], K.ident[:, :])
                    lastt.then_inc(s_t, 1)
                if isinstance(j, int) and j == 0:
                    pe.wait_ge(K.s_wpl, 32)
                pe.wait_ge(s_hT, 3 * j + 1)
                wait_if(pe, s_gm, 2 * j)
                for b in range(2):
                    for k in range(KP):
                        lastt = nc.tensor.matmul(Q[b][:, :], pT[:, k, :], wp[:, k, ts(b, 512)],
                                                 start=(k == 0), stop=(k == KP - 1))
                    lastt.then_inc(s_q, 1)
                pe.wait_ge(s_hT, 3 * j + 3)
                for b in range(2):
                    for k in range(KD):
                        lastt = nc.tensor.matmul(G[b][:, :], hT[:, k, :], wg[:, k, ts(b, 512)],
                                                 start=(k == 0), stop=(k == KD - 1))
                    lastt.then_inc(s_g, 1)
            lag1(pe, Chain(pe, c_x[2]), step)

        @block.vector
        def _(dve):
            c = Chain(dve, c_dve)
            dve.wait_ge(s_c, 32)

            def step(j, now, last):
                if now:
                    dve.wait_ge(s_ld, 32 * j + 32)
                    dve.wait_ge(s_y, 32 * j + 32)
                    if last:
                        c.sync()
                    c.mark(nc.vector.scalar_tensor_tensor(x3[:, :], y[0][:, :], K.wts[:, 0, ds(j, 1)], x2[:, :],
                                                          ALU.mult, ALU.add))
                    c.sync()
                    nc.vector.scalar_tensor_tensor(x3[:, :], y[1][:, :], K.wts[:, 1, ds(j, 1)], x3[:, :],
                                                   ALU.mult, ALU.add).then_inc(s_x3, 1)
                    dve.wait_ge(s_rstd, j + 1)
                    wait_if(dve, s_t, 3 * j)
                    nc.vector.scalar_tensor_tensor(h3[:, :], x3[:, :], rstd[:, 0:1], gain[:, :],
                                                   ALU.mult, ALU.mult).then_inc(s_h, 1)
                if last:
                    for b in range(2):
                        dve.wait_ge(s_g, 2 * (j - 1) + b + 1)
                        nc.vector.tensor_tensor(gt[:, ts(b, 512)], G[b][:, :], bg[:, ts(b, 512)],
                                                ALU.add).then_inc(s_ga, 1)
                    dve.wait_ge(s_gs, j)
                    for b in range(2):
                        nc.vector.tensor_tensor(gt[:, ts(b, 512)], Q[b][:, :], gt[:, ts(b, 512)],
                                                ALU.mult).then_inc(s_gm, 1)
                    dve.wait_ge(s_gm, 2 * j)
                    dve.wait_ge(s_st, 16 * j)
                    nc.vector.tensor_tensor(o[:, :], gt[:, :], keep[:, :], ALU.add).then_inc(s_o, 1)
                if now:
                    if last:
                        dve.wait_ge(s_o, j)
                    c.mark(nc.vector.tensor_copy(keep[:, :], x3[:, :]))
                    c.sync()
            lag1(dve, c, step)


class Keep:
    pass


def build(nc, inputs, out, stop=9, kind=None):
    K = Keep()
    K.x, K.p, K.attn_norm_g = inputs["x"], inputs["p"], inputs["attn_norm_g"]
    K.w_in, K.q_norm_g, K.k_norm_g = inputs["w_in"], inputs["q_norm_g"], inputs["k_norm_g"]
    K.cmp_pos, K.cmp_w1, K.cmp_w2 = inputs["cmp_pos"], inputs["cmp_w1"], inputs["cmp_w2"]
    K.w_attn_out, K.conv_w, K.conv_b = inputs["w_attn_out"], inputs["conv_w"], inputs["conv_b"]
    K.conv_norm_g, K.conv_norm_b, K.w_conv_out = inputs["conv_norm_g"], inputs["conv_norm_b"], inputs["w_conv_out"]
    K.merge_b, K.w_out, K.ffn_norm_g = inputs["merge_b"], inputs["w_out"], inputs["ffn_norm_g"]
    K.w_router_group, K.b_router_group, K.w_router_expert = inputs["w_router_group"], inputs["b_router_group"], inputs["w_router_expert"]
    K.b_router_expert, K.w_exp_gate, K.w_exp_up = inputs["b_router_expert"], inputs["w_exp_gate"], inputs["w_exp_up"]
    K.w_exp_down, K.ple_norm_g, K.w_ple_gate = inputs["w_exp_down"], inputs["ple_norm_g"], inputs["w_ple_gate"]
    K.b_ple_gate, K.w_ple_proj = inputs["b_ple_gate"], inputs["w_ple_proj"]
    K.out = out

    def scratch(name, shape):
        return (nc.dram_tensor(name, shape, F32, kind=kind) if kind else nc.dram_tensor(name, shape, F32)).ap()
    K.hT_d, K.q_d = scratch("hT_d", [NT, P, KD, P]), scratch("q_d", [NT, P, NH * AUG])
    K.zT_d, K.oT_d = scratch("zT_d", [CONV, ZT_COLS]), scratch("oT_d", [NT, P, KF, P])
    K.x2_d, K.h2_d, K.y_d = scratch("x2_d", [SEQ, D]), scratch("h2_d", [SEQ, D]), scratch("y_d", [MAX_BLK * P, D])
    with ExitStack() as ctx:
        sb, _ = bufs(nc, ctx)
        K.ident, K.identb = sb("ident", [P, P]), sb("identb", [P, P], BF16)
        K.mhalf, K.tpos = sb("minus_half", [P, 16]), sb("token_pos", [P, NT])
        K.inv_d, K.inv_hd = sb("inv_d", [P, 16]), sb("inv_hd", [P, 16])
        K.lg = sb("router_logits", [P, NT, NG + NE])
        K.idx, K.slots = sb("idx", [P, MAX_BLK + 1], U32), sb("slots", [P, 2, NT], U32)
        K.starts, K.wts = sb("block_starts", [1, NE + 1], I32), sb("expert_weights", [P, 2, NT])
        K.s_wm = nc.alloc_semaphore("w_merge_loaded")
        mrg = ctx.enter_context(ExitStack())
        with ExitStack() as att:
            sb, _ = bufs(nc, att)
            K.m_old, K.m_causal = sb("m_old", [P, P], BF16), sb("m_causal", [P, 2 * QB - P], BF16)
            K.mT_old, K.mT_causal = sb("mT_old", [P, P], BF16), sb("mT_causal", [P, 2 * QB - P], BF16)
            K.m_cmp, K.has_cmp = sb("m_cmp", [P, NEGC + P], BF16), sb("has_cmp", [P, NT])
            K.nslope = sb("minus_slope", [P, NH])
            K.forced, K.valid = sb("forced", [P, 2 * NSB - 2]), sb("valid", [P, 2 * NSB - 2])
            K.kselT, K.kwinT = sb("kselT", [P, NKV, SEQ]), sb("kwinT", [96, NKV, WINDOW + SEQ])
            K.vsel, K.vwin = sb("vsel", [P, NT, NKV, HD + 1]), sb("vwin", [P, WINDOW // P + NT, NKV, HD + 1])
            K.kcT, K.vc = sb("kcT", [96, NKV, P]), sb("vc", [P, NKV, HD])
            K.gates = sb("branch_gates", [P, NT, 3 * NH])
            with ExitStack() as raw:
                sb, _ = bufs(nc, raw)
                K.kvT = sb("kvT", [P, 2, SEQ])
                with ExitStack() as pro:
                    K.w_proj = bufs(nc, pro)[0]("w_proj", [P, KD, OFF_MERGE])
                    K.s_w = [nc.alloc_semaphore(f"w_proj{n}") for n in range(len(CHUNKS))]
                    make_constants(nc, K)
                    project(nc, K)
                if stop > 1:
                    compress(nc, K)
            sb, _ = bufs(nc, att)
            K.zero_row, K.s_zero = sb("zero_row", [P, D]), nc.alloc_semaphore("zeros_stored")
            K.wm = [mrg.enter_context(nc.sbuf_tensor("w_merge0", [P, KD, D], F32, side="right"))]
            K.keyA, K.keyB = sb("keyA", [P, NKV, SEQ], F32R), sb("keyB", [P, NKV, SEQ], F32R)
            if stop > 2:
                split_keys(nc, K)
                for quarter in range(4):
                    attend(nc, K, quarter)
        if stop > 3:
            K.wm.append(mrg.enter_context(nc.sbuf_tensor("w_merge1", [P, KD, D], F32, side="right")))
            merge(nc, K)
            mrg.close()
        if stop > 4:
            sb, _ = bufs(nc, ctx)
            K.wpg, K.wpp = sb("w_ple_gate", [P, KD, D]), sb("w_ple_proj", [P, PLE // P, D])
            K.s_wpl = nc.alloc_semaphore("w_ple_loaded")
            with ExitStack() as moe:
                sb, _ = bufs(nc, moe)
                K.wg = [sb(f"w_gate{i}", [P, KD, FF]) for i in range(2)]
                K.wu = [sb(f"w_up{i}", [P, KD, FF]) for i in range(2)]
                K.wd = [sb(f"w_down{i}", [P, KF, D]) for i in range(2)]
                K.s_gu = [nc.alloc_semaphore(f"gate_up_loaded{i}") for i in range(2)]
                K.s_wd = [nc.alloc_semaphore(f"down_loaded{i}") for i in range(2)]
                route(nc, K)
                experts(nc, K)
            combine(nc, K)


_INS = ["x", "p", "attn_norm_g", "w_in", "q_norm_g", "k_norm_g", "cmp_pos", "cmp_w1", "cmp_w2", "w_attn_out",
        "conv_w", "conv_b", "conv_norm_g", "conv_norm_b", "w_conv_out", "merge_b", "w_out", "ffn_norm_g",
        "w_router_group", "b_router_group", "w_router_expert", "b_router_expert", "w_exp_gate", "w_exp_up",
        "w_exp_down", "ple_norm_g", "w_ple_gate", "b_ple_gate", "w_ple_proj"]


def kernel(**inputs):
    import numpy as _np
    import concourse.bacc as _bacc
    from concourse import mybir as _mybir
    from concourse.bass_utils import run_bass_kernel_spmd as _run

    nc = _bacc.Bacc("TRN2", target_bir_lowering=False, num_devices=1)
    arrays, aps = {}, {}
    for name in _INS:
        a = _np.ascontiguousarray(inputs[name])
        arrays[f"in_{name}"] = a
        aps[name] = nc.dram_tensor(f"in_{name}", a.shape, _mybir.dt.from_np(a.dtype), kind="ExternalInput").ap()
    out = nc.dram_tensor("out_x", (1, SEQ, D), F32, kind="ExternalOutput").ap()
    build(nc, aps, out)
    r = _run(nc, [arrays], core_ids=[0])
    return r.results[0]["out_x"]
```
